# Optimizing a Trainium2 kernel written in Bass

```python
import math
import jax, jax.numpy as jnp
from jax import lax
import numpy as np

D_MODEL = 1024
BATCH = 1
SEQ = 512
DEPTH = 2

N_MIXERS = 2
EPS = 1e-6
POOL_WINDOWS = (2, 4, 8, 16)
N_POOL_GROUPS = len(POOL_WINDOWS)
POOL_GROUP_DIM = D_MODEL // N_POOL_GROUPS
HEAD_DIM = 64
N_HEADS = D_MODEL // HEAD_DIM
D_ATTN = N_HEADS * HEAD_DIM
ATTN_PATTERNS = ((128, 1), (512, 4), (2048, 16))
N_ATTN_GROUPS = len(ATTN_PATTERNS)
HEAD_GROUPS = tuple(N_HEADS // N_ATTN_GROUPS + (1 if g < N_HEADS % N_ATTN_GROUPS else 0) for g in range(N_ATTN_GROUPS))
ROPE_THETA = 10000.0
D_FF = -(-8 * D_MODEL // (3 * 256)) * 256
N_POOL_LAYERS = (DEPTH + 1) // 2
N_ATTN_LAYERS = DEPTH // 2
NEG_INF = -1e30


def rmsnorm(x, g):
    xf = x.astype(jnp.float32)
    y = xf * lax.rsqrt(jnp.mean(xf * xf, axis=-1, keepdims=True) + EPS)
    return (y * g.astype(jnp.float32)).astype(x.dtype)

def rope(t):
    S, hd = t.shape[1], t.shape[-1]
    inv_freq = 1.0 / (ROPE_THETA ** (jnp.arange(0, hd, 2, dtype=jnp.float32) / hd))
    ang = jnp.arange(S, dtype=jnp.float32)[:, None] * inv_freq[None, :]
    ang = jnp.concatenate([ang, ang], axis=-1)[None, :, None, :]
    tf = t.astype(jnp.float32)
    t1, t2 = tf[..., : hd // 2], tf[..., hd // 2 :]
    rot = jnp.concatenate([-t2, t1], axis=-1)
    return (tf * jnp.cos(ang) + rot * jnp.sin(ang)).astype(t.dtype)

def pool_mixer(h, w_in, w_group, scale, w_out):
    B, S, _ = h.shape
    u = jnp.einsum('bsd,de->bse', h, w_in).reshape(B, S, N_POOL_GROUPS, POOL_GROUP_DIM)
    cs = jnp.cumsum(u.astype(jnp.float32), axis=1)
    pos = jnp.arange(S)
    outs = []
    for g, w in enumerate(POOL_WINDOWS):
        c = cs[:, :, g]
        lag = jnp.pad(c, ((0, 0), (w, 0), (0, 0)))[:, :S]
        cnt = jnp.minimum(pos + 1, w).astype(jnp.float32)[None, :, None]
        outs.append((c - lag) / cnt - u[:, :, g].astype(jnp.float32))
    p = jnp.stack(outs, axis=2).astype(h.dtype)
    z = jnp.einsum('bsgc,gce->bsge', p, w_group).reshape(B, S, D_MODEL) * scale
    return jnp.einsum('bsd,de->bse', z, w_out)

def dilated_window_attention(q, k, v, window, dilation):
    B, S, H, hd = q.shape
    w = window // dilation
    L = S // dilation
    nb = -(-L // w)
    Lp = nb * w

    def to_blocks(t):
        t = t.reshape(B, L, dilation, H, hd)
        t = jnp.pad(t, ((0, 0), (0, Lp - L), (0, 0), (0, 0), (0, 0)))
        return t.reshape(B, nb, w, dilation, H, hd)

    qb, kb, vb = to_blocks(q), to_blocks(k), to_blocks(v)

    def with_prev(t):
        prev = jnp.concatenate([jnp.zeros_like(t[:, :1]), t[:, :-1]], axis=1)
        return jnp.concatenate([prev, t], axis=2)

    kc, vc = with_prev(kb), with_prev(vb)
    s = jnp.einsum('bnqrhd,bnkrhd->bnrhqk', qb, kc).astype(jnp.float32)
    qi = jnp.arange(w)[:, None]
    kj = jnp.arange(2 * w)[None, :]
    dist = w + qi - kj
    key_idx = jnp.arange(nb)[:, None, None] * w - w + kj[None]
    mask = (dist >= 0)[None] & (dist <= w)[None] & (key_idx >= 0)
    s = jnp.where(mask[None, :, None, None], s, NEG_INF)
    m = jnp.max(s, axis=-1, keepdims=True)
    e = jnp.exp(s - m)
    den = jnp.sum(e, axis=-1, keepdims=True)
    p = (e / den).astype(v.dtype)
    o = jnp.einsum('bnrhqk,bnkrhd->bnqrhd', p, vc)
    lse = (m + jnp.log(den))[..., 0]
    lse = jnp.transpose(lse, (0, 1, 4, 2, 3))
    o = o.reshape(B, Lp, dilation, H, hd)[:, :L].reshape(B, S, H, hd)
    lse = lse.reshape(B, Lp, dilation, H)[:, :L].reshape(B, S, H)
    return o, lse

def attn_mixer(h, w_qkv, w_out):
    B, S, _ = h.shape
    qkv = jnp.einsum('bsd,de->bse', h, w_qkv).reshape(B, S, 3, N_HEADS, HEAD_DIM)
    q = rope(qkv[:, :, 0]) * jnp.asarray(HEAD_DIM ** -0.5, dtype=h.dtype)
    k = rope(qkv[:, :, 1])
    v = qkv[:, :, 2]
    outs, lses = [], []
    start = 0
    for (window, dilation), n_g in zip(ATTN_PATTERNS, HEAD_GROUPS):
        sl = slice(start, start + n_g)
        o_g, lse_g = dilated_window_attention(q[:, :, sl], k[:, :, sl], v[:, :, sl], window, dilation)
        outs.append(o_g)
        lses.append(jax.nn.logsumexp(lse_g, axis=-1) - math.log(n_g))
        start += n_g
    alpha = jax.nn.softmax(jnp.stack(lses, axis=-1), axis=-1)
    merged = jnp.concatenate(
        [o_g * (N_ATTN_GROUPS * alpha[:, :, g]).astype(o_g.dtype)[:, :, None, None] for g, o_g in enumerate(outs)],
        axis=2,
    ).reshape(B, S, D_ATTN)
    return jnp.einsum('bse,ed->bsd', merged, w_out)

def swiglu(h, w_gate, w_up, w_down):
    g = jnp.einsum('bsd,df->bsf', h, w_gate)
    u = jnp.einsum('bsd,df->bsf', h, w_up)
    return jnp.einsum('bsf,fd->bsd', jax.nn.silu(g) * u, w_down)

def first_inputs(seed: int = 0) -> dict:
    key = jax.random.key(seed)
    ks = jax.random.split(key, 14)
    f32 = jnp.float32
    nrm = lambda k, shape, fan_in: jax.random.normal(k, shape, f32) * (fan_in ** -0.5)
    return {
        "x": jax.random.normal(ks[0], (BATCH, SEQ, D_MODEL), f32),
        "norm_mix": 1.0 + 0.05 * jax.random.normal(ks[1], (DEPTH, D_MODEL), f32),
        "norm_ffn": 1.0 + 0.05 * jax.random.normal(ks[2], (DEPTH, D_MODEL), f32),
        "norm_final": 1.0 + 0.05 * jax.random.normal(ks[3], (D_MODEL,), f32),
        "pool_w_in": nrm(ks[4], (N_POOL_LAYERS, D_MODEL, D_MODEL), D_MODEL),
        "pool_w_group": nrm(ks[5], (N_POOL_LAYERS, N_POOL_GROUPS, POOL_GROUP_DIM, POOL_GROUP_DIM), POOL_GROUP_DIM),
        "pool_scale": 1.0 + 0.1 * jax.random.normal(ks[6], (N_POOL_LAYERS, D_MODEL), f32),
        "pool_w_out": nrm(ks[7], (N_POOL_LAYERS, D_MODEL, D_MODEL), D_MODEL),
        "attn_w_qkv": nrm(ks[8], (N_ATTN_LAYERS, D_MODEL, 3 * D_ATTN), D_MODEL),
        "attn_w_out": nrm(ks[9], (N_ATTN_LAYERS, D_ATTN, D_MODEL), D_ATTN),
        "ffn_w_gate": nrm(ks[10], (DEPTH, D_MODEL, D_FF), D_MODEL),
        "ffn_w_up": nrm(ks[11], (DEPTH, D_MODEL, D_FF), D_MODEL),
        "ffn_w_down": nrm(ks[12], (DEPTH, D_FF, D_MODEL), D_FF),
    }

def first_block(x, norm_mix, norm_ffn, norm_final, pool_w_in, pool_w_group, pool_scale, pool_w_out,
              attn_w_qkv, attn_w_out, ffn_w_gate, ffn_w_up, ffn_w_down):
    for i in range(DEPTH):
        h = rmsnorm(x, norm_mix[i])
        j = i // N_MIXERS
        if i % N_MIXERS == 0:
            y = pool_mixer(h, pool_w_in[j], pool_w_group[j], pool_scale[j], pool_w_out[j])
        else:
            y = attn_mixer(h, attn_w_qkv[j], attn_w_out[j])
        x = x + y
        h = rmsnorm(x, norm_ffn[i])
        x = x + swiglu(h, ffn_w_gate[i], ffn_w_up[i], ffn_w_down[i])
    return rmsnorm(x, norm_final)


MIX_WIDTH = D_MODEL
SGU_CHUNK = 128
SGU_WIDTH = MIX_WIDTH // 2
SGU_GROUPS = 4
SGU_GROUP_DIM = SGU_WIDTH // SGU_GROUPS
ATT_WIDTH = MIX_WIDTH - SGU_WIDTH
ATT_HEAD_DIM = 64
ATT_HEADS = ATT_WIDTH // ATT_HEAD_DIM
IDX_HEADS = 4
IDX_HEAD_DIM = 64
TOPK_MAX = 256
ROPE_THETA_2 = 500000.0
ROPE_FRACTION = 4
D_FF_2 = 2816
Q_BLOCK = 128
RMS_EPS = 1e-6
N_MOD = 9

OFF_SGU_U = 0
OFF_SGU_V = OFF_SGU_U + SGU_WIDTH
OFF_Q = OFF_SGU_V + SGU_WIDTH
OFF_K = OFF_Q + ATT_WIDTH
OFF_V = OFF_K + ATT_WIDTH
OFF_IQ = OFF_V + ATT_WIDTH
OFF_IK = OFF_IQ + IDX_HEADS * IDX_HEAD_DIM
OFF_IW = OFF_IK + IDX_HEAD_DIM
PROJ_WIDTH = OFF_IW + IDX_HEADS


def rms_norm(x, g):
    xf = x.astype(jnp.float32)
    y = xf * lax.rsqrt(jnp.mean(xf * xf, axis=-1, keepdims=True) + RMS_EPS)
    return (y * g.astype(jnp.float32)).astype(x.dtype)

def modulate(h, shift, scale):
    return h * (1 + scale[:, None, :]) + shift[:, None, :]

def swiglu_2(h, w_in, w_out):
    g, u = jnp.split(h @ w_in, 2, axis=-1)
    return (jax.nn.silu(g) * u) @ w_out

def rope_tables(positions, rot_dim):
    inv_freq = ROPE_THETA_2 ** (-jnp.arange(0, rot_dim, 2, dtype=jnp.float32) / rot_dim)
    ang = positions.astype(jnp.float32)[..., None] * inv_freq
    return jnp.cos(ang)[:, :, None, :], jnp.sin(ang)[:, :, None, :]

def partial_rope(x, cos, sin):
    half = cos.shape[-1]
    rot = 2 * half
    xr = x[..., :rot].astype(jnp.float32)
    x1, x2 = xr[..., :half], xr[..., half:]
    out = jnp.concatenate([x1 * cos - x2 * sin, x2 * cos + x1 * sin], axis=-1).astype(x.dtype)
    return jnp.concatenate([out, x[..., rot:]], axis=-1)

def chunked_sgu(u, v, w_s, b_s):
    B, S, _ = u.shape
    n_chunk = S // SGU_CHUNK
    v = v.reshape(B, n_chunk, SGU_CHUNK, SGU_GROUPS, SGU_GROUP_DIM)
    causal = jnp.tril(jnp.ones((SGU_CHUNK, SGU_CHUNK), dtype=bool))
    w = jnp.where(causal[None], w_s, 0).astype(v.dtype)
    mixed = jnp.einsum('gts,bnsgc->bntgc', w, v) + b_s.T[None, None, :, :, None].astype(v.dtype)
    return u * mixed.reshape(B, S, SGU_WIDTH)

def dsa_attention(q, k, v, qi, ki, wi):
    B, S = q.shape[0], q.shape[1]
    top_k = min(TOPK_MAX, S // 4)
    n_blk = S // Q_BLOCK

    def to_blocks(a):
        return a.reshape((B, n_blk, Q_BLOCK) + a.shape[2:]).swapaxes(0, 1)

    t_blocks = jnp.arange(S, dtype=jnp.int32).reshape(n_blk, Q_BLOCK)
    key_pos = jnp.arange(S, dtype=jnp.int32)
    ki_f = ki.astype(jnp.float32)
    scale = ATT_HEAD_DIM ** -0.5

    def one_block(args):
        qb, qib, wib, tb = args
        logits = jax.nn.relu(jnp.einsum('bqhd,bsd->bqhs', qib.astype(jnp.float32), ki_f))
        score = jnp.einsum('bqh,bqhs->bqs', wib.astype(jnp.float32), logits)
        causal = key_pos[None, :] <= tb[:, None]
        score = jnp.where(causal[None], score, -jnp.inf)
        _, idx = lax.top_k(score, top_k)
        valid = idx <= tb[None, :, None]
        kg = jax.vmap(lambda kb, ib: kb[ib])(k, idx)
        vg = jax.vmap(lambda vb, ib: vb[ib])(v, idx)
        s = jnp.einsum('bqhd,bqkhd->bhqk', qb, kg).astype(jnp.float32) * scale
        s = jnp.where(valid[:, None], s, -jnp.inf)
        p = jax.nn.softmax(s, axis=-1).astype(vg.dtype)
        return jnp.einsum('bhqk,bqkhd->bqhd', p, vg)

    out = lax.map(one_block, (to_blocks(q), to_blocks(qi), to_blocks(wi), t_blocks))
    return out.swapaxes(0, 1).reshape(B, S, ATT_WIDTH)

def token_mix(h, cos, sin, w_in, sgu_w, sgu_b, w_out):
    B, S, _ = h.shape
    p = h @ w_in
    u = jax.nn.gelu(p[..., OFF_SGU_U:OFF_SGU_V], approximate=False)
    va = jax.nn.gelu(p[..., OFF_SGU_V:OFF_Q], approximate=False)
    a_out = chunked_sgu(u, va, sgu_w, sgu_b)
    q = partial_rope(p[..., OFF_Q:OFF_K].reshape(B, S, ATT_HEADS, ATT_HEAD_DIM), cos, sin)
    k = partial_rope(p[..., OFF_K:OFF_V].reshape(B, S, ATT_HEADS, ATT_HEAD_DIM), cos, sin)
    v = p[..., OFF_V:OFF_IQ].reshape(B, S, ATT_HEADS, ATT_HEAD_DIM)
    qi = partial_rope(p[..., OFF_IQ:OFF_IK].reshape(B, S, IDX_HEADS, IDX_HEAD_DIM), cos, sin)
    ki = partial_rope(p[..., OFF_IK:OFF_IW][:, :, None, :], cos, sin)[:, :, 0, :]
    wi = p[..., OFF_IW:PROJ_WIDTH]
    b_out = dsa_attention(q, k, v, qi, ki, wi)
    return jnp.concatenate([a_out, b_out], axis=-1) @ w_out

def second_inputs(seed: int = 0) -> dict:
    key = jax.random.key(seed)
    ks = jax.random.split(key, 24)
    f32 = jnp.float32
    L, D = DEPTH, D_MODEL

    def nrm(k, shape, scale):
        return jax.random.normal(k, shape, f32) * scale

    x = jax.random.normal(ks[0], (BATCH, SEQ, D), f32)
    c = jax.random.normal(ks[1], (BATCH, D), f32)
    positions = (jnp.arange(SEQ, dtype=jnp.int32)[None, :]
                 + jax.random.randint(ks[2], (BATCH, 1), 0, 4096, dtype=jnp.int32))
    return {
        "x": x,
        "c": c,
        "positions": positions,
        "ada_w": nrm(ks[3], (L, D, N_MOD * D), 0.5 * D ** -0.5),
        "ada_b": nrm(ks[4], (L, N_MOD * D), 0.01),
        "norm_ffn1": 1.0 + nrm(ks[5], (L, D), 0.02),
        "ffn1_w_in": nrm(ks[6], (L, D, 2 * D_FF_2), D ** -0.5),
        "ffn1_w_out": nrm(ks[7], (L, D_FF_2, D), D_FF_2 ** -0.5),
        "norm_mix": 1.0 + nrm(ks[8], (L, D), 0.02),
        "mix_w_in": nrm(ks[9], (L, D, PROJ_WIDTH), D ** -0.5),
        "sgu_w": nrm(ks[10], (L, SGU_GROUPS, SGU_CHUNK, SGU_CHUNK), SGU_CHUNK ** -0.5),
        "sgu_b": 1.0 + nrm(ks[11], (L, SGU_GROUPS, SGU_CHUNK), 0.02),
        "mix_w_out": nrm(ks[12], (L, MIX_WIDTH, D), MIX_WIDTH ** -0.5),
        "norm_ffn2": 1.0 + nrm(ks[13], (L, D), 0.02),
        "ffn2_w_in": nrm(ks[14], (L, D, 2 * D_FF_2), D ** -0.5),
        "ffn2_w_out": nrm(ks[15], (L, D_FF_2, D), D_FF_2 ** -0.5),
        "final_norm": 1.0 + nrm(ks[16], (D,), 0.02),
    }

def second_block(x, c, positions, ada_w, ada_b, norm_ffn1, ffn1_w_in, ffn1_w_out,
              norm_mix, mix_w_in, sgu_w, sgu_b, mix_w_out,
              norm_ffn2, ffn2_w_in, ffn2_w_out, final_norm):
    cos, sin = rope_tables(positions, ATT_HEAD_DIM // ROPE_FRACTION)
    cos, sin = cos.astype(x.dtype), sin.astype(x.dtype)
    c_act = jax.nn.silu(c)
    for l in range(DEPTH):
        mod = c_act @ ada_w[l] + ada_b[l]
        sh1, sc1, g1, sh2, sc2, g2, sh3, sc3, g3 = jnp.split(mod, N_MOD, axis=-1)
        h = modulate(rms_norm(x, norm_ffn1[l]), sh1, sc1)
        x = x + 0.5 * g1[:, None, :] * swiglu_2(h, ffn1_w_in[l], ffn1_w_out[l])
        h = modulate(rms_norm(x, norm_mix[l]), sh2, sc2)
        x = x + g2[:, None, :] * token_mix(h, cos, sin, mix_w_in[l], sgu_w[l], sgu_b[l], mix_w_out[l])
        h = modulate(rms_norm(x, norm_ffn2[l]), sh3, sc3)
        x = x + 0.5 * g3[:, None, :] * swiglu_2(h, ffn2_w_in[l], ffn2_w_out[l])
    return rms_norm(x, final_norm)


def setup_inputs(seed=0):
    out = dict(first_inputs(seed))
    for name, value in second_inputs(seed + 1).items():
        if name != "x":
            out[name + "_2"] = value
    return out


def reference(
    x, norm_mix, norm_ffn, norm_final, pool_w_in, pool_w_group, pool_scale, pool_w_out,
    attn_w_qkv, attn_w_out, ffn_w_gate, ffn_w_up, ffn_w_down, c_2, positions_2, ada_w_2,
    ada_b_2, norm_ffn1_2, ffn1_w_in_2, ffn1_w_out_2, norm_mix_2, mix_w_in_2, sgu_w_2, sgu_b_2,
    mix_w_out_2, norm_ffn2_2, ffn2_w_in_2, ffn2_w_out_2, final_norm_2,
):
    x = first_block(
        x, norm_mix, norm_ffn, norm_final, pool_w_in, pool_w_group, pool_scale, pool_w_out,
        attn_w_qkv, attn_w_out, ffn_w_gate, ffn_w_up, ffn_w_down,
    )
    return second_block(
        x, c_2, positions_2, ada_w_2, ada_b_2, norm_ffn1_2, ffn1_w_in_2, ffn1_w_out_2,
        norm_mix_2, mix_w_in_2, sgu_w_2, sgu_b_2, mix_w_out_2, norm_ffn2_2, ffn2_w_in_2,
        ffn2_w_out_2, final_norm_2,
    )


_drawn_inputs = setup_inputs


def setup_inputs(seed=0):
    import zlib

    import numpy as np

    out = dict(_drawn_inputs(seed))
    spreads = {}
    factors = {'ada_b_2': 3.999,
     'norm_ffn1_2': 8.0,
     'norm_mix_2': 6.584,
     'sgu_b_2': 8.0,
     'norm_ffn2_2': 8.0,
     'final_norm_2': 2.73}
    for name, (base, spread) in spreads.items():
        noise = np.random.default_rng([zlib.crc32(name.encode()), seed]).standard_normal(out[name].shape)
        drawn = base * np.exp(spread * noise) if base else spread * noise
        out[name] = __import__('jax').numpy.asarray(drawn.astype(out[name].dtype))
    for name, factor in factors.items():
        out[name] = (out[name] * factor).astype(out[name].dtype)
    return out
```

```python
from contextlib import ExitStack

import numpy as np

import concourse.bass as bass
from concourse import mybir

P = 128
S = 512
D = 1024
KC = D // P
NB = S // P
DFF = 2816
NF = DFF // P
HD = 64
EPS = 1e-6
NEG = -1e30
TAKEN = -3e38
SLAB = 1024
RAW = 4
SPL = 2

F32 = mybir.dt.float32
FR = mybir.dt.float32r
I32 = mybir.dt.int32
ACT = mybir.ActivationFunctionType
ALU = mybir.AluOpType
AX_X = mybir.AxisListType.X

POOL_WINDOWS = (2, 4, 8, 16)
HEAD_GROUPS = ((0, 6), (6, 11), (11, 16))
TOPK = 128
SGU_GROUPS = 4
IDX_HEADS = 4
N_MOD = 9
OFF_U, OFF_VA, OFF_Q, OFF_K, OFF_V, OFF_IQ, OFF_IK, OFF_IW = 0, 512, 1024, 1536, 2048, 2560, 2816, 2880

VEC_ROWS = {}
_at = 0
for _name, _n in (("norm_mix", 16), ("norm_ffn", 16), ("norm_final", 8), ("pool_scale", 8), ("c", 8),
                  ("f1", 16), ("mix2", 16), ("f2", 16), ("final2", 8)):
    VEC_ROWS[_name] = _at
    _at += _n
N_VEC = _at

TRI = [64 * b * (b + 1) for b in range(NB + 1)]


def constants():
    ident = np.eye(P, dtype=np.float32)
    half_turn = np.zeros((P, P), np.float32)
    part_turn = np.zeros((P, P), np.float32)
    for h in (0, HD):
        for d in range(HD // 2):
            half_turn[h + d + HD // 2, h + d] = -1.0
            half_turn[h + d, h + d + HD // 2] = 1.0
        for d in range(HD // 8):
            part_turn[h + d + HD // 8, h + d] = -1.0
            part_turn[h + d, h + d + HD // 8] = 1.0
    upper = np.triu(np.ones((P, P), np.float32))
    squares = np.concatenate([ident, half_turn, part_turn, upper], 1)

    f1 = (1.0 / (np.float32(10000.0) ** (np.arange(0, HD, 2, dtype=np.float32) / np.float32(HD)))).astype(np.float32)
    ang = (np.arange(S, dtype=np.float32)[None, :] * f1[:, None]).astype(np.float32)
    ang = np.tile(ang, (4, 1)).astype(np.float64)
    rope = np.concatenate([np.cos(ang), np.sin(ang)], 1).astype(np.float32)

    q = np.arange(S)[:, None]
    k = np.arange(S)[None, :]
    rules = [(q >= k) & (q - k <= 128), (q >= k) & ((q - k) % 4 == 0), (q >= k) & ((q - k) % 16 == 0), q >= k]
    masks = np.zeros((4, P, TRI[NB]), np.float32)
    for n, rule in enumerate(rules):
        bias = np.where(rule, 0.0, NEG).astype(np.float32)
        for b in range(NB):
            masks[n, :, TRI[b]:TRI[b + 1]] = bias[b * P:(b + 1) * P, :(b + 1) * P]

    t = np.arange(16)
    ratio = np.stack([w / np.minimum(t + 1, w) for w in POOL_WINDOWS]).astype(np.float32)
    small = np.zeros((P, 67), np.float32)
    small[:, :64] = ratio.reshape(1, 64)
    rot = HD // 4
    f2 = np.float32(500000.0) ** (-np.arange(0, rot, 2, dtype=np.float32) / np.float32(rot))
    for h in (0, HD):
        small[h:h + rot // 2, 64] = f2
        small[h + rot // 2:h + rot, 64] = f2
    small[:, 65] = EPS
    small[:, 66] = 1.0
    return squares, rope, masks, small


def two_pi_parts():
    left, parts = 2.0 * np.pi, []
    for bits in (9, 9, 9):
        e = np.floor(np.log2(left))
        step = 2.0 ** (e - bits + 1)
        c = np.floor(left / step) * step
        parts.append(float(c))
        left -= c
    parts.append(float(np.float32(left)))
    return parts


def program(nc, x, norm_mix, norm_ffn, norm_final, pool_w_in, pool_w_group, pool_scale, pool_w_out,
            attn_w_qkv, attn_w_out, ffn_w_gate, ffn_w_up, ffn_w_down, c_2, positions_2, ada_w_2, ada_b_2,
            norm_ffn1_2, ffn1_w_in_2, ffn1_w_out_2, norm_mix_2, mix_w_in_2, sgu_w_2, sgu_b_2, mix_w_out_2,
            norm_ffn2_2, ffn2_w_in_2, ffn2_w_out_2, final_norm_2, squares_c, rope_c, masks_c, small_c, out):
    with ExitStack() as ctx:
        arena_at = (nc.sbuf_base + 31) // 32 * 32
        ctx.enter_context(nc.sbuf_tensor("arena", [P, 212480 // 4], F32))
        cursor = [arena_at]

        def place(name, shape, dt=F32, at=None):
            size = int(np.prod(shape[1:])) * 4
            if at is None:
                at = cursor[0]
                cursor[0] += (size + 31) // 32 * 32
                assert cursor[0] <= arena_at + 212480, (name, cursor[0] - arena_at)
            return nc.alloc_sbuf_tensor_at(name, shape, dt, offset=at)

        xT = place("xT", [P, KC, S])
        h_hi = place("h_hi", [P, KC, S], FR)
        h_lo = place("h_lo", [P, KC, S], FR)
        raw = place("raw", [P, RAW, SLAB])
        w_hi = place("w_hi", [P, SPL, SLAB], FR)
        w_lo = place("w_lo", [P, SPL, SLAB], FR)
        ada_w = place("ada_w", [P, 2, 4, 512])
        ada_acc = place("ada_acc", [P, 512])
        sumsq = place("sumsq", [P, S])
        sq = place("sq", [P, 2, S])
        rstd = place("rstd", [P, S])
        work = place("work", [P, 4, S])
        vec = place("vec", [P, N_VEC])
        adab = place("adab", [P, 2 * N_MOD * KC])
        mod = place("mod", [P, 2 * N_MOD * KC])
        coefs = place("coefs", [P, 2, 5, KC])
        squares = place("squares", [P, 4, P])
        small = place("small", [P, 67])
        ones = place("ones", [P, P])
        cact = place("cact", [P, KC])
        scratch1 = place("scratch1", [P, 1])
        reg = cursor[0]
        REG_END = reg + 2 * NF * S * 4
        assert REG_END <= arena_at + 212480, REG_END - arena_at
        ident, half_turn, part_turn, upper = (squares[:, i, :] for i in range(4))

        act_hi = place("act_hi", [P, NF, S], FR, at=reg)
        act_lo = place("act_lo", [P, NF, S], FR, at=reg + NF * S * 4)

        def layout(prefix, items):
            at, got = reg, {}
            for name, shape, dt in items:
                got[name] = place(prefix + name, shape, dt, at=at)
                at += (int(np.prod(shape[1:])) * 4 + 31) // 32 * 32
            assert at <= REG_END, (prefix, at - REG_END)
            return got

        x_nat = place("x_nat", [P, NB, D], at=reg + 8 * S * 4)
        vrows = place("vrows", [P, P], at=reg + 16 * S * 4)
        brows = place("brows", [P, 2, P], at=reg + 16 * S * 4 + 512)
        uP = place("uP", [P, 8, S], at=reg + 8 * S * 4 + NF * S * 4)
        winA = place("winA", [P, 2, S], at=reg + 17 * S * 4)
        pP = place("pP", [P, 2, S], at=reg + 19 * S * 4)

        a1 = layout("a1_", [("qT", [P, 8, S], F32), ("kT", [P, 8, S], F32), ("vN", [P, NB, D], F32),
                            ("oN", [P, NB, D], F32), ("masks", [P, 3, TRI[NB]], F32),
                            ("P", [P, 2, S], F32), ("PT", [P, 2, S], F32), ("nmx", [P, 64], F32), ("den", [P, 64], F32)])
        o_at = reg + 3 * 8 * S * 4
        a1["stage"] = place("a1_stage", [P, 4, S], at=o_at)
        a1["cos"] = place("a1_cos", [P, 2, S], at=o_at + 4 * S * 4)
        a1["tmp"] = place("a1_tmp", [P, 2, S], at=o_at + 6 * S * 4)
        fine = place("fine", [P, 6, NB, 16], at=reg)

        a2 = layout("a2_", [("qT", [P, 4, S], F32), ("kT", [P, 4, S], F32), ("vN", [P, NB, 512], F32),
                            ("oN", [P, NB, 512], F32), ("uT", [P, 4, S], F32), ("vaN", [P, NB, 512], F32),
                            ("score", [P, TRI[NB]], F32), ("causal", [P, TRI[NB]], F32), ("masks", [P, 1, TRI[NB]], F32),
                            ("cos", [P, 2, S], F32), ("tmp", [P, 2, S], F32), ("stage", [P, 4, S], F32),
                            ("sguw", [P, 4, P], F32), ("wT", [P, 4, P], F32), ("bbc", [P, 4, P], F32),
                            ("nmx", [P, 32], F32), ("den", [P, 32], F32), ("wi", [P, NB, 4], F32),
                            ("iw", [P, KC, 4], F32), ("iwh", [P, KC, 4], FR), ("iwl", [P, KC, 4], FR),
                            ("m8", [P, 3, 8], F32)])
        o_at2 = reg + 3 * 4 * S * 4
        a2["iqT"] = place("a2_iqT", [P, 2, S], at=o_at2)
        a2["ikT"] = place("a2_ikT", [P, 1, S], at=o_at2 + 2 * S * 4)
        st_at = reg + (6 * 4 * S + 3 * TRI[NB] + 4 * S) * 4
        a2["P"] = place("a2_P", [P, 2, S], at=st_at)
        a2["PT"] = place("a2_PT", [P, 2, S], at=st_at + 2 * S * 4)
        yT = place("yT", [P, KC, S], at=reg)
        y_nat = place("y_nat", [P, NB, D], at=reg + KC * S * 4)

        bank = [ctx.enter_context(nc.psum_tensor(f"bank{i}", [P, S], F32)) for i in range(8)]

        def sem(name):
            return ctx.enter_context(nc.semaphore(name))

        s_const = sem("consts_loaded")
        s_vecs = sem("vectors_loaded")
        s_xin = [sem(f"x_block{b}_loaded") for b in range(NB)]
        s_load = [sem(f"slab_loaded_slot{j}") for j in range(RAW)]
        s_ik2 = sem("index_key_copy_loaded")
        s_hi = sem("slab_hi_ready")
        s_lo = sem("slab_lo_ready")
        s_used = sem("slab_used_by_pe")
        s_x = sem("x_chunk_ready")
        s_sq = sem("square_ready")
        s_sum = sem("square_added")
        s_mean = sem("mean_ready")
        s_sd = sem("deviation_ready")
        s_rstd = sem("rstd_ready")
        s_htmp = sem("normed_chunk_ready")
        s_hhi = sem("h_hi_ready")
        s_hlo = sem("h_lo_ready")
        s_actT = sem("tile_out_by_act")
        s_dveT = sem("tile_out_by_dve")
        s_down = sem("down_chunk_done")
        s_ahi = sem("act_hi_ready")
        s_alo = sem("act_lo_ready")
        s_adaload = [sem(f"ada_half{h}_loaded") for h in range(2)]
        s_adastep = sem("ada_partial_sum")
        s_adamm = sem("ada_reduced")
        s_mod = sem("modulation_ready")
        s_dve = sem("dve_step_done")
        s_act = sem("act_step_done")
        s_setup = sem("vectors_transposed")
        s_vec = sem("vectors_on_partitions")
        s_ones = sem("ones_ready")
        s_xtr = sem("x_transposed")
        s_win = sem("window_ready")
        s_phaseld = sem("mix_tables_loaded")
        s_postmm = sem("post_mm_done")
        s_post = sem("post_done")
        s_iw = sem("index_weights_mm")
        s_wi = sem("index_weights_ready")
        s_iwh = sem("index_w_hi")
        s_iwl = sem("index_w_lo")
        s_tab = sem("rope_angle_ready")
        s_sin = sem("rope_table_ready")
        s_wtr = sem("sgu_w_transposed")
        s_wT = sem("sgu_w_ready")
        s_idxmm = sem("index_scores_mm")
        s_relu = sem("index_relu_ready")
        s_idx = sem("index_score_added")
        s_mask = sem("topk_mask_ready")
        s_sgumm = sem("sgu_mm_done")
        s_sgu = sem("sgu_out_ready")
        s_scmm = sem("scores_mm")
        s_masked = sem("scores_masked")
        s_exp = sem("exp_done")
        s_tr = sem("probs_transposed")
        s_pt = sem("probsT_ready")
        s_pv = sem("pv_done")
        s_o = sem("o_out")
        s_aw = sem("alpha_exponent_ready")
        s_ae = sem("alpha_exp_done")
        s_on = sem("o_scaled")
        s_otr = sem("o_transposed")
        s_ytr = sem("y_transposed")
        s_ynat = sem("y_natural_ready")
        s_out = [sem(f"out_block{b}_stored") for b in range(NB)]

        def kview(w):
            return w.rearrange("(k p) c -> p k c", p=P)

        def pairs_of(w, col0, n_pairs):
            v = kview(w)
            return [v[:, 4 * half:4 * half + 4, col0 + 256 * j:col0 + 256 * j + 256]
                    for j in range(n_pairs) for half in range(2)]

        def down_slabs(w):
            v = kview(w)
            return [v[:, 2 * kk:2 * kk + 2, 512 * half:512 * half + 512] for half in range(2) for kk in range(NF // 2)]

        A1_GROUPS = [(2, [("v", 2 * j), ("v", 2 * j + 1)]) for j in range(4)]
        A1_GROUPS += [(2, [("k", 2 * j), ("k", 2 * j + 1)]) for j in range(4)]
        A1_GROUPS += [(2, [("q", 2 * j), ("q", 2 * j + 1)]) for j in range(4)]
        A2_GROUPS = [(2, [("iq", 0), ("iq", 1)]), (1, [("ik", 0)])]
        for kind in ("v", "k", "q", "va", "u"):
            A2_GROUPS += [(2, [(kind, 2 * j), (kind, 2 * j + 1)]) for j in range(2)]

        wg = pool_w_group[0].rearrange("g (k p) e -> p (g k) e", p=P)
        n_slabs = 0
        N0 = {}
        for name, n in [("pool_in", 8), ("group", 2), ("pool_out", 8), ("ffn0", 66), ("proj0", 24), ("out0", 8),
                        ("ffn1", 66), ("ffn2", 66), ("proj1", 23), ("out1", 8), ("ffn3", 66), ("ffn4", 66),
                        ("proj2", 23), ("out2", 8), ("ffn5", 66)]:
            N0[name] = n_slabs
            n_slabs += n

        gate_of = [ffn_w_gate[0], ffn_w_gate[1]] + [None] * 4
        up_of = [ffn_w_up[0], ffn_w_up[1]] + [None] * 4
        down_of = [ffn_w_down[0], ffn_w_down[1], ffn1_w_out_2[0], ffn2_w_out_2[0], ffn1_w_out_2[1], ffn2_w_out_2[1]]
        for f, w in ((2, ffn1_w_in_2[0]), (3, ffn2_w_in_2[0]), (4, ffn1_w_in_2[1]), (5, ffn2_w_in_2[1])):
            gate_of[f], up_of[f] = w[:, 0:DFF], w[:, DFF:2 * DFF]

        H0 = {name: 8 * i for i, name in enumerate(
            ["n0", "pool", "n1", "n2", "attn0", "n3", "n5", "n6", "attn1", "n7", "n8", "n9", "attn2", "n10"])}
        HT0 = {name: 8 * i for i, name in enumerate(["n0", "n1", "n2", "n3", "n5", "n6", "n7", "n8", "n9", "n10"])}
        OT0 = [0, 8, 12]
        ACT0 = {"pool": 0} | {f: 8 + NF * f for f in range(6)}
        ATT = [dict(nh=16, u0=0, hp0=0, b=a1), dict(nh=8, u0=64, hp0=8, b=a2), dict(nh=8, u0=96, hp0=12, b=a2)]
        for t in ATT:
            t["nu"] = 4 * t["nh"]
        AT0, DT0, a, d = {}, {}, 0, 0
        for name in N0:
            AT0[name], DT0[name] = a, d
            if name == "pool_in":
                a += 8
            elif name.startswith("ffn"):
                a += NF
                d += NF
            elif name.startswith("proj"):
                a += sum(len(t) for _, t in (A1_GROUPS if name == "proj0" else A2_GROUPS))
        PO0 = [0, 24, 24 + 19]

        block = ctx.enter_context(nc.Block())

        @block.sync
        def _(sp):
            def load(nb, src, i=0, shape=None):
                if nb >= RAW:
                    sp.wait_ge(s_lo, nb - RAW + 1 + 4 * i)
                dst = raw[:, nb % RAW, :].rearrange("p (k c) -> p k c", c=shape)
                return sp.dma_start(dst, src).then_inc(s_load[nb % RAW], 16)

            for b in range(NB):
                sp.dma_start(x_nat[:, b, :], x[0, b * P:(b + 1) * P, :]).then_inc(s_xin[b], 16)

            def load_list(name, srcs, c):
                for j, src in enumerate(srcs):
                    load(N0[name] + j, src, shape=c)

            def load_ffn(f):
                nb = N0[f"ffn{f}"]
                g, u = kview(gate_of[f]), kview(up_of[f])
                with sp.Fori(0, NF // 2) as i:
                    for j, w in enumerate((g, g, u, u)):
                        half = j % 2
                        load(nb + j, w[:, 4 * half:4 * half + 4, bass.ds(i * 256, 256)], i, shape=256)
                for j, src in enumerate(down_slabs(down_of[f])):
                    load(nb + 44 + j, src, shape=512)

            load_list("pool_in", pairs_of(pool_w_in[0], 0, 4), 256)
            load_list("group", [wg[:, 4 * j:4 * j + 4, :] for j in range(2)], 256)
            load_list("pool_out", pairs_of(pool_w_out[0], 0, 4), 256)
            load_ffn(0)
            load_list("proj0", pairs_of(attn_w_qkv[0], 2 * D, 4) + pairs_of(attn_w_qkv[0], D, 4)
                      + pairs_of(attn_w_qkv[0], 0, 4), 256)
            load_list("out0", pairs_of(attn_w_out[0], 0, 4), 256)
            load_ffn(1)
            for layer in range(2):
                load_ffn(2 + 2 * layer)
                w = mix_w_in_2[layer]
                name = f"proj{1 + layer}"
                nb = N0[name]
                for j, src in enumerate(pairs_of(w, OFF_IQ, 1)):
                    load(nb + j, src, shape=256)
                nk = nb + 2
                sp.wait_ge(s_lo, nk - RAW + 1)
                dst = raw[:, nk % RAW, :].rearrange("p (k c) -> p k c", c=P)
                ikw = kview(w)[:, :, OFF_IK:OFF_IK + HD]
                sp.dma_start(dst[:, :, 0:HD], ikw).then_inc(s_load[nk % RAW], 16)
                sp.dma_start(dst[:, :, HD:P], ikw).then_inc(s_ik2, 16)
                rest = []
                for off in (OFF_V, OFF_K, OFF_Q, OFF_VA, OFF_U):
                    rest += pairs_of(w, off, 2)
                for j, src in enumerate(rest):
                    load(nb + 3 + j, src, shape=256)
                load_list(f"out{1 + layer}", pairs_of(mix_w_out_2[layer], 0, 4), 256)
                load_ffn(3 + 2 * layer)
            for b in range(NB):
                sp.wait_ge(s_ynat, 2 * b + 2)
                sp.dma_start(out[0, b * P:(b + 1) * P, :], y_nat[:, b, :]).then_inc(s_out[b], 16)
            for b in range(NB):
                sp.wait_ge(s_out[b], 16)

        @block.gpsimd
        def _(pool):
            pool.dma_start(squares[:], squares_c.rearrange("p (n c) -> p n c", c=P)).then_inc(s_const, 16)
            pool.dma_start(small[:], small_c).then_inc(s_const, 16)
            vectors = [("norm_mix", norm_mix), ("norm_ffn", norm_ffn), ("pool_scale", pool_scale), ("c", c_2),
                       ("f1", norm_ffn1_2), ("mix2", norm_mix_2), ("f2", norm_ffn2_2)]
            for name, v in vectors:
                n = v.shape[0] * KC
                r = VEC_ROWS[name]
                pool.dma_start(vrows[r:r + n, :], v.rearrange("l (k p) -> (l k) p", p=P)).then_inc(s_vecs, 16)
            for name, v in (("norm_final", norm_final), ("final2", final_norm_2)):
                r = VEC_ROWS[name]
                pool.dma_start(vrows[r:r + KC, :], v.rearrange("(k p) -> k p", p=P)).then_inc(s_vecs, 16)
            for l in range(2):
                pool.dma_start(brows[0:N_MOD * KC, l, :],
                               ada_b_2[l].rearrange("(k p) -> k p", p=P)).then_inc(s_vecs, 16)

            def ada_loads(f):
                w = kview(ada_w_2[f // 2])

                def halves(i, first=False):
                    for half in range(2):
                        if not first:
                            pool.wait_ge(s_adastep, 8 * (N_MOD * f - 1) + 4 * half + 4 + 8 * i)
                        pool.dma_start(ada_w[:, half], w[:, 4 * half:4 * half + 4, bass.ds(i * 512 + (f % 2) * N_MOD * 512, 512)])\
                            .then_inc(s_adaload[half], 16)

                if f == 0:
                    halves(0, True)
                with pool.Fori(1 if f == 0 else 0, N_MOD) as i:
                    halves(i)

            def mix_tables(m):
                pool.wait_ge(s_used, N0[f"proj{m}"])
                if m == 0:
                    pool.dma_start(a1["cos"][:], rope_c.rearrange("p (n s) -> p n s", s=S)).then_inc(s_phaseld, 16)
                    for g in range(3):
                        pool.dma_start(a1["masks"][:, g, :], masks_c[g]).then_inc(s_phaseld, 16)
                    return
                l = m - 1
                pool.dma_start(a2["iw"][:], kview(mix_w_in_2[l])[:, :, OFF_IW:OFF_IW + IDX_HEADS]).then_inc(s_phaseld, 16)
                pool.dma_start(a2["stage"][:, 3, :].bitcast(I32), positions_2[0:1, :].to_broadcast([P, S]))\
                    .then_inc(s_phaseld, 16)
                pool.dma_start(a2["causal"][:], masks_c[3]).then_inc(s_phaseld, 16)
                pool.dma_start(a2["masks"][:, 0, 0:P], masks_c[3, :, 0:P]).then_inc(s_phaseld, 16)
                pool.dma_start(a2["sguw"][:], sgu_w_2[l].rearrange("g t s -> t g s")).then_inc(s_phaseld, 16)
                pool.dma_start(a2["bbc"][:].rearrange("p g t -> p (g t)"),
                               sgu_b_2[l].rearrange("g t -> (g t)")[None, :].to_broadcast([P, 4 * P]))\
                    .then_inc(s_phaseld, 16)

            ada_loads(0)
            mix_tables(0)
            ada_loads(1)
            ada_loads(2)
            mix_tables(1)
            ada_loads(3)
            mix_tables(2)

        PHASE_LD = [64, 64 + 96, 64 + 192]

        @block.scalar
        def _(act):
            steps = [0]

            def link(ins):
                steps[0] += 1
                ins.then_inc(s_act, 1)
                act.wait_ge(s_act, steps[0])

            def split_hi(nb, i=0):
                if nb >= n_slabs:
                    return
                act.wait_ge(s_load[nb % RAW], 16 * (nb // RAW + 1) + 16 * i)
                for m in (1, 2):
                    if nb == N0[f"proj{m}"] + 2:
                        act.wait_ge(s_ik2, 16 * m)
                if nb >= SPL:
                    act.wait_ge(s_used, nb - SPL + 1 + 4 * i)
                nc.scalar.activation(w_hi[:, nb % SPL, :], raw[:, nb % RAW, :], ACT.Copy).then_inc(s_hi, 1)

            def square_chunk(q, k):
                act.wait_ge(s_x, 8 * q + k + 1)
                n = 7 * q + k
                if k == 0:
                    if q:
                        act.wait_ge(s_sd, q)
                    nc.scalar.activation(sumsq[:], xT[:, 0, :], ACT.Square).then_inc(s_sq, 1)
                else:
                    if n - 1 >= 2:
                        act.wait_ge(s_sum, n - 2)
                    nc.scalar.activation(sq[:, (n - 1) % 2, :], xT[:, k, :], ACT.Square).then_inc(s_sq, 1)

            def norm_tail(q, hname, shift):
                nc.scalar.activation(scratch1[:], small[:, 65:66], ACT.Sqrt)
                act.wait_ge(s_mean, q + 1)
                nc.scalar.activation(rstd[:], bank[7][:], ACT.Sqrt, bias=small[:, 65:66]).then_inc(s_sd, 1)
                if hname is None:
                    return
                base = H0[hname]
                for k in range(KC):
                    act.wait_ge(s_htmp, HT0[hname] + k + 1)
                    if shift is None:
                        nc.scalar.activation(h_hi[:, k, :], work[:, k % 4, :], ACT.Copy).then_inc(s_hhi, 1)
                    else:
                        if k == 0:
                            act.wait_ge(s_mod, 18 if shift < 72 else 36)
                        nc.scalar.activation(h_hi[:, k, :], work[:, k % 4, :], ACT.Identity,
                                             bias=mod[:, shift + k:shift + k + 1]).then_inc(s_hhi, 1)

            def residual_squares(q, ks):
                for k in ks:
                    square_chunk(q, k)

            def ffn(f, q_next):
                nb, at, dt, aa = N0[f"ffn{f}"], AT0[f"ffn{f}"], DT0[f"ffn{f}"], ACT0[f]
                with act.Fori(0, NF // 2) as i:
                    split_hi(nb + 2, i)
                    split_hi(nb + 3, i)
                    for c in range(2):
                        act.wait_ge(s_used, nb + 2 + 4 * i)
                        nc.scalar.activation(work[:, c, :], bank[c][:], ACT.Silu).then_inc(s_actT, 1)
                    split_hi(nb + 4, i)
                    split_hi(nb + 5, i)
                    for c in range(2):
                        act.wait_ge(s_dveT, dt + c + 1 + 2 * i)
                        nc.scalar.activation(act_hi[:, bass.ds(i * 2 + c, 1), :], work[:, 2 + c:3 + c, :], ACT.Copy).then_inc(s_ahi, 1)
                for s in range(22):
                    split_hi(nb + 44 + s + 2)
                    if 12 <= s < 16:
                        square_chunk(q_next, s - 12)
                for k in range(4, 8):
                    square_chunk(q_next, k)

            def out_phase(name, q_next):
                nb = N0[name]
                for j in range(4):
                    split_hi(nb + 2 * j + 2)
                    split_hi(nb + 2 * j + 3)
                    residual_squares(q_next, (2 * j, 2 * j + 1))

            def project(m, groups, bufs):
                nb, at = N0[f"proj{m}"], AT0[f"proj{m}"]
                n, tile, staged = nb, 0, 0
                if m:
                    act.wait_ge(s_phaseld, PHASE_LD[m])
                    nc.scalar.activation(bufs["iwh"][:], bufs["iw"][:], ACT.Copy).then_inc(s_iwh, 1)
                    for j in range(2):
                        act.wait_ge(s_tab, 2 * (m - 1) + j + 1)
                        nc.scalar.activation(bufs["cos"][:, j, :], bufs["tmp"][:, j, :], ACT.Sin).then_inc(s_sin, 1)
                for g, (slabs, tiles) in enumerate(groups):
                    for j in range(slabs):
                        split_hi(n + 2 + j)
                    n += slabs
                    for kind, idx in tiles:
                        act.wait_ge(s_used, n)
                        src = bank[2 * (g % 2) + idx % 2][:]
                        if kind == "u":
                            nc.scalar.activation(bufs["uT"][:, idx, :], src, ACT.Gelu).then_inc(s_actT, 1)
                        else:
                            if staged >= 4:
                                act.wait_ge(s_post, PO0[m] + staged - 3)
                            elif m and staged == 3:
                                act.wait_ge(s_tab, 2 * m)
                            nc.scalar.activation(bufs["stage"][:, staged % 4, :], src,
                                                 ACT.Gelu if kind == "va" else ACT.Copy).then_inc(s_actT, 1)
                            staged += 1
                    if m and g == 1:
                        act.wait_ge(s_iw, m)
                        nc.scalar.activation(bufs["wi"][:].rearrange("p b h -> p (b h)"), bank[6][:, 0:16], ACT.Copy)\
                            .then_inc(s_wi, 1)
                    if m and 3 <= g <= 5:
                        for h in range(4):
                            x = 4 * (g - 3) + h
                            y = 12 * (m - 1) + x
                            b = g - 2
                            act.wait_ge(s_idxmm, y + 1)
                            if x >= 2:
                                act.wait_ge(s_idx, y - 1)
                            nc.scalar.activation(work[:, x % 2, 0:(b + 1) * P], bank[6 + x % 2][:, 0:(b + 1) * P],
                                                 ACT.Relu).then_inc(s_relu, 1)

            def attention(m):
                t = ATT[m]
                u0, b_ = t["u0"], t["b"]
                for u in range(t["nu"]):
                    b = u % 4
                    n = (b + 1) * P
                    act.wait_ge(s_masked, u0 + u + 1)
                    if u >= 2:
                        act.wait_ge(s_tr, u0 + u - 1)
                    nc.scalar.activation(b_["P"][:, u % 2, 0:n], bank[u % 2][:, 0:n], ACT.Exp, scale=-1.0,
                                         bias=b_["nmx"][:, u:u + 1], accum_out=b_["den"][:, u:u + 1]).then_inc(s_exp, 1)
                    if u % 8 == 3 and u >= 8:
                        o_out(t, u // 8 - 1)
                o_out(t, t["nh"] // 2 - 1)
                if m == 0:
                    act.wait_ge(s_aw, 1)
                    nc.scalar.activation(fine[:, 1], fine[:, 0], ACT.Exp).then_inc(s_ae, 1)
                c0 = 0 if m == 0 else 4
                for c in range(c0, KC):
                    o = OT0[m] + c - c0
                    act.wait_ge(s_otr, o + 1)
                    nc.scalar.activation(h_hi[:, c, :], bank[6 + c % 2][:], ACT.Copy).then_inc(s_hhi, 1)

            def o_out(t, hp):
                act.wait_ge(s_pv, t["u0"] + 8 * hp + 8)
                nc.scalar.activation(
                    t["b"]["oN"][:, :, hp * 2 * HD:(hp + 1) * 2 * HD].rearrange("p b (h d) -> p b h d", d=HD),
                    bank[4 + hp % 2][:].rearrange("p (h b d) -> p b h d", h=2, d=HD), ACT.Copy).then_inc(s_o, 1)

            split_hi(0)
            split_hi(1)
            act.wait_ge(s_setup, 1)
            link(nc.scalar.activation(vec[:], bank[4][:, 0:N_VEC], ACT.Copy))
            nc.scalar.activation(adab[:], bank[5][:, 0:2 * N_MOD * KC], ACT.Copy)
            nc.scalar.activation(cact[:], vec[:, VEC_ROWS["c"]:VEC_ROWS["c"] + KC], ACT.Silu).then_inc(s_vec, 1)
            residual_squares(0, range(8))
            norm_tail(0, "n0", None)

            nb = N0["pool_in"]
            for j in range(4):
                split_hi(nb + 2 * j + 2)
                split_hi(nb + 2 * j + 3)
                for c in (2 * j, 2 * j + 1):
                    act.wait_ge(s_used, nb + 2 * j + 2)
                    nc.scalar.activation(uP[:, c, :], bank[c % 4][:], ACT.Copy).then_inc(s_actT, 1)
            act.wait_ge(s_used, nb + 8)
            for c in range(8):
                act.wait_ge(s_win, c + 1)
                nc.scalar.activation(h_hi[:, c, :], pP[:, c % 2, :], ACT.Copy).then_inc(s_hhi, 1)
            nb = N0["group"]
            for j in range(2):
                split_hi(nb + j + 2)
                for c in range(4 * j, 4 * j + 4):
                    act.wait_ge(s_used, nb + j + 1)
                    r = VEC_ROWS["pool_scale"] + c
                    nc.scalar.activation(act_hi[:, c, :], bank[c][:], ACT.Identity, scale=vec[:, r:r + 1]).then_inc(s_ahi, 1)
            out_phase("pool_out", 1)
            norm_tail(1, "n1", None)
            ffn(0, 2)
            norm_tail(2, "n2", None)
            project(0, A1_GROUPS, a1)
            attention(0)
            out_phase("out0", 3)
            norm_tail(3, "n3", None)
            ffn(1, 4)
            norm_tail(4, None, None)
            residual_squares(5, range(8))
            norm_tail(5, "n5", 0)
            for l in range(2):
                q = 5 + 3 * l
                ffn(2 + 2 * l, q + 1)
                norm_tail(q + 1, ["n6", "n9"][l], 72 * l + 24)
                project(1 + l, A2_GROUPS, a2)
                for g in range(SGU_GROUPS):
                    act.wait_ge(s_sgu, 4 * l + g + 1)
                    nc.scalar.activation(h_hi[:, g, :], work[:, 2 + g % 2, :], ACT.Copy).then_inc(s_hhi, 1)
                attention(1 + l)
                out_phase(f"out{1 + l}", q + 2)
                norm_tail(q + 2, ["n7", "n10"][l], 72 * l + 48)
                ffn(3 + 2 * l, q + 3)
                if l == 0:
                    norm_tail(8, "n8", 72)
            norm_tail(11, None, None)

        @block.vector
        def _(dve):
            steps = [0]
            V = nc.vector

            def link(ins):
                steps[0] += 1
                ins.then_inc(s_dve, 1)
                dve.wait_ge(s_dve, steps[0])

            def split_lo(nb, i=0):
                if nb >= n_slabs:
                    return
                dve.wait_ge(s_hi, nb + 1 + 4 * i)
                V.tensor_tensor(w_lo[:, nb % SPL, :], raw[:, nb % RAW, :], w_hi[:, nb % SPL, :].bitcast(F32),
                                ALU.subtract).then_inc(s_lo, 1)

            def add_square(q, k):
                if k == 0:
                    return
                dve.wait_ge(s_sq, 8 * q + k + 1)
                if k > 1:
                    dve.wait_ge(s_sum, 7 * q + k - 1)
                V.tensor_tensor(sumsq[:], sumsq[:], sq[:, (7 * q + k - 1) % 2, :], ALU.add).then_inc(s_sum, 1)

            def norm_tail(q, hname, gains, shift=None):
                dve.wait_ge(s_sd, q + 1)
                V.reciprocal(rstd[:], rstd[:]).then_inc(s_rstd, 1)
                dve.wait_ge(s_rstd, q + 1)
                if hname is None:
                    dst = xT if q == 4 else yT
                    for k in range(KC):
                        V.scalar_tensor_tensor(out=dst[:, k, :], in0=xT[:, k, :], scalar=gains[:, k:k + 1], in1=rstd[:],
                                               op0=ALU.mult, op1=ALU.mult).then_inc(s_x, 1)
                    return
                base, ht = H0[hname], HT0[hname]
                for k in range(KC + 1):
                    if k < KC:
                        if k >= 4:
                            dve.wait_ge(s_hlo, base + k - 3)
                        V.scalar_tensor_tensor(out=work[:, k % 4, :], in0=xT[:, k, :], scalar=gains[:, k:k + 1],
                                               in1=rstd[:], op0=ALU.mult, op1=ALU.mult).then_inc(s_htmp, 1)
                    if k:
                        c = k - 1
                        dve.wait_ge(s_hhi, base + c + 1)
                        sh = 0.0 if shift is None else mod[:, shift + c:shift + c + 1]
                        V.scalar_tensor_tensor(out=h_lo[:, c, :], in0=work[:, c % 4, :], scalar=sh,
                                               in1=h_hi[:, c, :].bitcast(F32), op0=ALU.add, op1=ALU.subtract)\
                            .then_inc(s_hlo, 1)

            def residual(c, src, gate):
                V.scalar_tensor_tensor(out=xT[:, c, :], in0=src, scalar=1.0 if gate is None else gate[:, c:c + 1],
                                       in1=xT[:, c, :], op0=ALU.mult, op1=ALU.add).then_inc(s_x, 1)

            def ffn(f, q_next, gate):
                nb, at, dt, aa = N0[f"ffn{f}"], AT0[f"ffn{f}"], DT0[f"ffn{f}"], ACT0[f]

                def ada_half(i, half):
                    dve.wait_ge(s_adaload[half], 16 * (N_MOD * f + 1) + 16 * i)
                    for j in range(4):
                        k = 4 * half + j
                        if k:
                            dve.wait_ge(s_adastep, 8 * N_MOD * f + k + 8 * i)
                        w = ada_w[:, half, j, :]
                        if k == 0:
                            ins = V.tensor_scalar(ada_acc[:], w, cact[:, 0:1], None, ALU.mult)
                        else:
                            ins = V.scalar_tensor_tensor(out=ada_acc[:], in0=w, scalar=cact[:, k:k + 1], in1=ada_acc[:],
                                                         op0=ALU.mult, op1=ALU.add)
                        ins.then_inc(s_adastep, 1)

                def body(i, ada):
                    split_lo(nb + 2, i)
                    if ada:
                        ada_half(i, 0)
                    split_lo(nb + 3, i)
                    if ada:
                        ada_half(i, 1)
                    split_lo(nb + 4, i)
                    split_lo(nb + 5, i)
                    dve.wait_ge(s_alo, aa + 2 * i)
                    for c in range(2):
                        dve.wait_ge(s_used, nb + 4 + 4 * i)
                        dve.wait_ge(s_actT, at + c + 1 + 2 * i)
                        V.tensor_tensor(work[:, 2 + c, :], work[:, c, :], bank[2 + c][:], ALU.mult).then_inc(s_dveT, 1)
                    for c in range(2):
                        dve.wait_ge(s_ahi, aa + c + 1 + 2 * i)
                        V.tensor_tensor(act_lo[:, bass.ds(i * 2 + c, 1), :], work[:, 2 + c:3 + c, :],
                                        act_hi[:, bass.ds(i * 2 + c, 1), :].bitcast(F32), ALU.subtract).then_inc(s_alo, 1)
                    if ada:
                        dve.wait_ge(s_adamm, N_MOD * f + 1 + i)
                        V.tensor_tensor(mod[:, bass.ds(i * 4 + 4 * N_MOD * f, 4)], bank[6][:, 0:4],
                                        adab[:, bass.ds(i * 4 + 4 * N_MOD * f, 4)], ALU.add).then_inc(s_mod, 1)

                if f < 4:
                    with dve.Fori(0, N_MOD) as i:
                        body(i, True)
                    with dve.Fori(N_MOD, NF // 2) as i:
                        body(i, False)
                else:
                    with dve.Fori(0, NF // 2) as i:
                        body(i, False)
                if f == 1:
                    modulation_gains(0)
                if f == 3:
                    modulation_gains(1)

                def down_done(half, c):
                    if c < 3:
                        dve.wait_ge(s_down, 6 * f + 3 * half + c + 1)
                    else:
                        dve.wait_ge(s_used, nb + 44 + 11 * (half + 1))

                for s in range(22):
                    split_lo(nb + 44 + s + 2)
                    if 11 <= s < 15:
                        c = s - 11
                        down_done(0, c)
                        residual(c, bank[4 + c][:], gate)
                    if 12 <= s < 16:
                        add_square(q_next, s - 12)
                for c in range(4, 8):
                    down_done(1, c - 4)
                    residual(c, bank[c - 4][:], gate)
                    if c > 4:
                        add_square(q_next, c - 1)
                add_square(q_next, 7)

            def modulation_gains(l):
                m = 72 * l
                dve.wait_ge(s_mod, 18 * (l + 1))
                for n, (vecname, sc) in enumerate((("f1", 8), ("mix2", 32), ("f2", 56))):
                    r = VEC_ROWS[vecname] + 8 * l
                    V.scalar_tensor_tensor(out=coefs[:, l, n, :], in0=mod[:, m + sc:m + sc + 8], scalar=1.0,
                                           in1=vec[:, r:r + 8], op0=ALU.add, op1=ALU.mult)
                V.tensor_scalar(coefs[:, l, 3, :], mod[:, m + 16:m + 24], 0.5, None, ALU.mult)
                link(V.tensor_scalar(coefs[:, l, 4, :], mod[:, m + 64:m + 72], 0.5, None, ALU.mult))

            def out_phase(name, q_next, gate):
                nb, dt = N0[name], DT0[name]
                for j in range(4):
                    split_lo(nb + 2 * j + 2)
                    split_lo(nb + 2 * j + 3)
                    for c in (2 * j, 2 * j + 1):
                        dve.wait_ge(s_used, nb + 2 * j + 2)
                        residual(c, bank[c % 4][:], gate)
                        if c:
                            add_square(q_next, c - 1)
                add_square(q_next, 7)

            def rope_tables(m, bufs):
                pi = float(np.float32(3.1415925))
                pos = bufs["stage"][:, 3, :]
                ang, t, r = bufs["stage"][:, 0, :], bufs["stage"][:, 1, :], bufs["stage"][:, 2, :]
                link(V.tensor_copy(t, pos.bitcast(I32)))
                link(V.tensor_scalar(ang, t, small[:, 64:65], None, ALU.mult))
                magic = 1.5 * 2.0 ** 23
                for j, quarter in enumerate((0.25, 0.0)):
                    link(V.tensor_scalar(t, ang, 1.0 / (2.0 * np.pi), quarter, ALU.mult, ALU.add))
                    link(V.tensor_scalar(t, t, magic, None, ALU.add))
                    link(V.tensor_scalar(t, t, -magic, None, ALU.add))
                    if j:
                        dve.wait_ge(s_tab, 2 * m - 1)
                    src = ang
                    for part in two_pi_parts():
                        link(V.scalar_tensor_tensor(out=r, in0=t, scalar=-part, in1=src, op0=ALU.mult, op1=ALU.add))
                        src = r
                    if quarter:
                        link(V.tensor_scalar(r, r, float(np.pi / 2), None, ALU.add))
                    V.tensor_scalar(bufs["tmp"][:, j, :], r, pi, -pi, ALU.min, ALU.max).then_inc(s_tab, 1)

            def project(m, groups, bufs):
                nb = N0[f"proj{m}"]
                n, post = nb, [0]
                pending = []
                dve.wait_ge(s_phaseld, PHASE_LD[m])
                if m:
                    rope_tables(m, bufs)
                    dve.wait_ge(s_iwh, m)
                    V.tensor_tensor(bufs["iwl"][:], bufs["iw"][:], bufs["iwh"][:].bitcast(F32), ALU.subtract)\
                        .then_inc(s_iwl, 1)

                def posts(tiles):
                    for kind, idx in tiles:
                        j = post[0]
                        post[0] += 1
                        src, aux = bufs["stage"][:, j % 4, :], bank[4 + j % 2]
                        if kind in ("v", "va"):
                            dve.wait_ge(s_postmm, PO0[m] + j + 1)
                            dst = bufs["vN" if kind == "v" else "vaN"][:, :, idx * P:(idx + 1) * P]
                            V.tensor_copy(dst, aux[:].rearrange("p (b d) -> p b d", d=P)).then_inc(s_post, 1)
                            continue
                        dst = bufs[kind + "T"][:, idx, :]
                        dve.wait_ge(s_actT, AT0[f"proj{m}"] + tile_of(j) + 1)
                        if m:
                            dve.wait_ge(s_sin, 2 * m)
                        if j >= 2:
                            dve.wait_ge(s_post, PO0[m] + j - 1)
                        V.tensor_tensor(dst, src, bufs["cos"][:, 0, :], ALU.mult)
                        dve.wait_ge(s_postmm, PO0[m] + j + 1)
                        link(V.tensor_tensor(bufs["tmp"][:, j % 2, :], aux[:], bufs["cos"][:, 1, :], ALU.mult))
                        V.tensor_tensor(dst, dst, bufs["tmp"][:, j % 2, :], ALU.add).then_inc(s_post, 1)

                order = [t for _, ts in groups for t in ts]

                def tile_of(j):
                    return [i for i, (kind, _) in enumerate(order) if kind != "u"][j]

                rounds = [3, 3, 3, 3, 2, 2]
                for g, (slabs, tiles) in enumerate(groups):
                    for j in range(slabs):
                        split_lo(n + 2 + j)
                    n += slabs
                    posts([t for t in pending if t[0] != "u"])
                    pending = tiles
                    if m and g == 2:
                        dve.wait_ge(s_wtr, m)
                        V.tensor_tensor(bufs["wT"][:], bank[7][:].rearrange("p (g t) -> p g t", t=P),
                                        upper.unsqueeze(1).to_broadcast([P, 4, P]), ALU.mult).then_inc(s_wT, 1)
                    if m and 3 <= g <= 5:
                        b = g - 2
                        w = bufs["score"][:, TRI[b]:TRI[b + 1]]
                        for h in range(4):
                            y = 12 * (m - 1) + 4 * (g - 3) + h
                            dve.wait_ge(s_relu, y + 1)
                            if h == 0:
                                dve.wait_ge(s_wi, m)
                            else:
                                dve.wait_ge(s_idx, y)
                            V.scalar_tensor_tensor(out=w, in0=work[:, (4 * (g - 3) + h) % 2, 0:(b + 1) * P],
                                                   scalar=bufs["wi"][:, b, h:h + 1],
                                                   in1=bufs["causal"][:, TRI[b]:TRI[b + 1]] if h == 0 else w,
                                                   op0=ALU.mult, op1=ALU.add).then_inc(s_idx, 1)
                    if m and g >= 6:
                        if g == 6:
                            dve.wait_ge(s_idx, 12 * m)
                        for _ in range(rounds[g - 6]):
                            topk_round(bufs)
                posts([t for t in pending if t[0] != "u"])
                if m:
                    for b in range(1, NB):
                        V.tensor_scalar(bufs["masks"][:, 0, TRI[b]:TRI[b + 1]], bufs["score"][:, TRI[b]:TRI[b + 1]],
                                        -2e38, NEG, ALU.is_gt, ALU.mult).then_inc(s_mask, 1)
                    dve.wait_ge(s_mask, 3 * m)
                    sgu(m, bufs)

            def topk_round(bufs):
                for b in range(1, NB):
                    ins = V.max(bufs["m8"][:, b - 1, :], bufs["score"][:, TRI[b]:TRI[b + 1]])
                    steps[0] += 1
                    ins.then_inc(s_dve, 1)
                for b in range(1, NB):
                    dve.wait_ge(s_dve, steps[0] - NB + 1 + b)
                    w = bufs["score"][:, TRI[b]:TRI[b + 1]]
                    ins = V.match_replace(out=w, in_to_replace=bufs["m8"][:, b - 1, :], in_values=w, imm_value=TAKEN)
                    ins.then_inc(s_dve, 1)
                steps[0] += NB - 1
                dve.wait_ge(s_dve, steps[0])

            def sgu(m, bufs):
                for g in range(SGU_GROUPS):
                    dve.wait_ge(s_sgumm, 4 * (m - 1) + g + 1)
                    dve.wait_ge(s_actT, AT0[f"proj{m}"] + 20 + g)
                    dst = work[:, 2 + g % 2, :]
                    if g >= 2:
                        dve.wait_ge(s_hlo, H0[f"attn{m}"] + g - 1)
                    link(V.tensor_tensor(dst.rearrange("p (n t) -> p n t", t=P), bank[6 + g % 2][:].rearrange("p (n t) -> p n t", t=P),
                                         bufs["bbc"][:, g:g + 1, :].to_broadcast([P, NB, P]), ALU.add))
                    V.tensor_tensor(dst, dst, bufs["uT"][:, g, :], ALU.mult).then_inc(s_sgu, 1)
                    dve.wait_ge(s_hhi, H0[f"attn{m}"] + g + 1)
                    V.tensor_tensor(h_lo[:, g, :], dst, h_hi[:, g, :].bitcast(F32), ALU.subtract).then_inc(s_hlo, 1)

            def attention(m):
                t = ATT[m]
                u0, bufs, nu, nh = t["u0"], t["b"], t["nu"], t["nh"]

                def mask_scores(u):
                    h, b = u // 4, u % 4
                    n = (b + 1) * P
                    g = [i for i, (lo, hi) in enumerate(HEAD_GROUPS) if lo <= h < hi][0] if m == 0 else 0
                    dve.wait_ge(s_scmm, u0 + u + 1)
                    V.tensor_tensor_reduce(out=bank[u % 2][:, 0:n], in0=bank[u % 2][:, 0:n],
                                           in1=bufs["masks"][:, g, TRI[b]:TRI[b + 1]], scale=-(HD ** -0.5), scalar=3e38,
                                           op0=ALU.add, op1=ALU.min, accum_out=bufs["nmx"][:, u:u + 1]).then_inc(s_masked, 1)

                mask_scores(0)
                mask_scores(1)
                for u in range(nu):
                    n = (u % 4 + 1) * P
                    dve.wait_ge(s_tr, u0 + u + 1)
                    if u >= 2:
                        dve.wait_ge(s_pv, u0 + u - 1)
                    V.tensor_copy(bufs["PT"][:, u % 2, 0:n], bank[2 + u % 2][:, 0:n]).then_inc(s_pt, 1)
                    if u + 2 < nu:
                        mask_scores(u + 2)
                den = bufs["den"][:, 0:nu].rearrange("p (h b) -> p b h", b=NB)
                nmx = bufs["nmx"][:, 0:nu].rearrange("p (h b) -> p b h", b=NB)
                dve.wait_ge(s_exp, u0 + nu)
                F = fine
                if m == 0:
                    least, ex, wsum, tot = F[:, 2, :, 0:1], F[:, 1], F[:, 3, :, 0:3], F[:, 4, :, 0:1]
                    link(V.tensor_reduce(least, nmx, AX_X, ALU.min))
                    V.tensor_tensor(F[:, 0], least.to_broadcast([P, NB, 16]), nmx, ALU.subtract).then_inc(s_aw, 1)
                    dve.wait_ge(s_ae, 1)
                    link(V.tensor_tensor(ex, ex, den, ALU.mult))
                    for g, (lo, hi) in enumerate(HEAD_GROUPS):
                        link(V.tensor_reduce(F[:, 3, :, g:g + 1], ex[:, :, lo:hi], AX_X, ALU.add))
                        link(V.tensor_scalar(F[:, 3, :, g:g + 1], F[:, 3, :, g:g + 1], 1.0 / (hi - lo), None, ALU.mult))
                    link(V.tensor_reduce(tot, wsum, AX_X, ALU.add))
                    link(V.reciprocal(tot, tot))
                    link(V.tensor_scalar(tot, tot, float(len(HEAD_GROUPS)), None, ALU.mult))
                    link(V.tensor_tensor(wsum, wsum, tot.to_broadcast([P, NB, 3]), ALU.mult))
                    link(V.reciprocal(F[:, 5], den))
                    for g, (lo, hi) in enumerate(HEAD_GROUPS):
                        link(V.tensor_tensor(F[:, 5, :, lo:hi], F[:, 5, :, lo:hi],
                                             F[:, 3, :, g:g + 1].to_broadcast([P, NB, hi - lo]), ALU.mult))
                    coef = F[:, 5]
                else:
                    link(V.reciprocal(F[:, 5, :, 0:nh], den))
                    coef = F[:, 5, :, 0:nh]
                dve.wait_ge(s_o, t["hp0"] + nh // 2)
                for b in range(NB):
                    o = bufs["oN"][:, b, :].rearrange("p (h d) -> p h d", d=HD)
                    V.tensor_tensor(o, o, coef[:, b, :].unsqueeze(2).to_broadcast([P, nh, HD]), ALU.mult).then_inc(s_on, 1)
                c0 = 0 if m == 0 else 4
                for c in range(c0, KC):
                    dve.wait_ge(s_hhi, H0[f"attn{m}"] + c + 1)
                    V.tensor_tensor(h_lo[:, c, :], bank[6 + c % 2][:], h_hi[:, c, :].bitcast(F32), ALU.subtract).then_inc(s_hlo, 1)

            V.memset(ones[:], 1.0 / D).then_inc(s_ones, 1)
            for k in range(KC):
                dve.wait_ge(s_xtr, k + 1)
                V.tensor_copy(xT[:, k, :], bank[k % 4][:]).then_inc(s_x, 1)
                add_square(0, k - 1) if k else None
            add_square(0, 7)
            split_lo(0)
            split_lo(1)
            dve.wait_ge(s_vec, 1)

            def gain(name, l=0):
                r = VEC_ROWS[name] + 8 * l
                return vec[:, r:r + 8]

            norm_tail(0, "n0", gain("norm_mix", 0))
            nb = N0["pool_in"]

            def window(c):
                g = c // 2
                dve.wait_ge(s_actT, c + 1)
                if c:
                    dve.wait_ge(s_win, c)
                src = uP[:, c, :]
                for j in range(g + 1):
                    sh, dst = 2 ** j, winA[:, j % 2, :]
                    V.tensor_copy(dst[:, 0:sh], src[:, 0:sh])
                    link(V.tensor_tensor(dst[:, sh:S], src[:, sh:S], src[:, 0:S - sh], ALU.add))
                    src = dst
                link(V.tensor_tensor(src[:, 0:16], src[:, 0:16], small[:, 16 * g:16 * g + 16], ALU.mult))
                if c >= 2:
                    dve.wait_ge(s_hhi, H0["pool"] + c - 1)
                V.scalar_tensor_tensor(out=pP[:, c % 2, :], in0=src, scalar=1.0 / POOL_WINDOWS[g], in1=uP[:, c, :],
                                       op0=ALU.mult, op1=ALU.subtract).then_inc(s_win, 1)

            def pool_lo(c):
                dve.wait_ge(s_hhi, H0["pool"] + c + 1)
                V.tensor_tensor(h_lo[:, c, :], pP[:, c % 2, :], h_hi[:, c, :].bitcast(F32), ALU.subtract).then_inc(s_hlo, 1)

            for j in range(4):
                split_lo(nb + 2 * j + 2)
                split_lo(nb + 2 * j + 3)
                if j == 1:
                    window(0)
                    window(1)
            for c in range(KC):
                if c >= 2:
                    window(c)
                pool_lo(c)
            nb = N0["group"]
            for j in range(2):
                split_lo(nb + j + 2)
                for c in range(4 * j, 4 * j + 4):
                    dve.wait_ge(s_ahi, c + 1)
                    r = VEC_ROWS["pool_scale"] + c
                    V.scalar_tensor_tensor(out=act_lo[:, c, :], in0=bank[c][:], scalar=vec[:, r:r + 1],
                                           in1=act_hi[:, c, :].bitcast(F32), op0=ALU.mult, op1=ALU.subtract).then_inc(s_alo, 1)
            out_phase("pool_out", 1, None)
            norm_tail(1, "n1", gain("norm_ffn", 0))
            ffn(0, 2, None)
            norm_tail(2, "n2", gain("norm_mix", 1))
            project(0, A1_GROUPS, a1)
            attention(0)
            out_phase("out0", 3, None)
            norm_tail(3, "n3", gain("norm_ffn", 1))
            ffn(1, 4, None)
            norm_tail(4, None, gain("norm_final"))
            for k in range(1, KC):
                add_square(5, k)
            norm_tail(5, "n5", coefs[:, 0, 0, :], 0)
            for l in range(2):
                q = 5 + 3 * l
                ffn(2 + 2 * l, q + 1, coefs[:, l, 3, :])
                norm_tail(q + 1, ["n6", "n9"][l], coefs[:, l, 1, :], 72 * l + 24)
                project(1 + l, A2_GROUPS, a2)
                attention(1 + l)
                out_phase(f"out{1 + l}", q + 2, mod[:, 72 * l + 40:72 * l + 48])
                norm_tail(q + 2, ["n7", "n10"][l], coefs[:, l, 2, :], 72 * l + 48)
                ffn(3 + 2 * l, q + 3, coefs[:, l, 4, :])
                if l == 0:
                    norm_tail(8, "n8", coefs[:, 1, 0, :], 72)
            norm_tail(11, None, gain("final2"))
            for b in range(NB):
                for half in range(2):
                    n = 2 * b + half
                    dve.wait_ge(s_ytr, n + 1)
                    V.tensor_copy(y_nat[:, b, 512 * half:512 * half + 512], bank[n % 4][:]).then_inc(s_ynat, 1)

        @block.tensor
        def _(pe):
            T = nc.tensor

            def mm3(dst, wh, wl, mh, ml, first, last):
                T.matmul(dst, wh, mh, start=first, stop=False)
                T.matmul(dst, wh, ml, start=False, stop=False)
                return T.matmul(dst, wl, mh, start=False, stop=last)

            def slab(nb, c):
                return (w_hi[:, nb % SPL, :].rearrange("p (k c) -> p k c", c=c),
                        w_lo[:, nb % SPL, :].rearrange("p (k c) -> p k c", c=c))

            def pair(nb, banks, mh, ml, ready=None, i=0, first_chunk=0):
                for half in range(2):
                    hi, lo = slab(nb + half, 256)
                    pe.wait_ge(s_lo, nb + half + 1 + 4 * i)
                    for c in range(2):
                        for j in range(4):
                            k = 4 * half + j
                            if ready is not None and c == 0:
                                pe.wait_ge(ready[0], ready[1] + k + 1)
                            ins = mm3(bank[banks[c]][:], hi[:, j, c * P:(c + 1) * P], lo[:, j, c * P:(c + 1) * P],
                                      mh[:, k, :], ml[:, k, :], k == 0, k == KC - 1)
                    ins.then_inc(s_used, 1)

            def mean(q):
                pe.wait_ge(s_sum, 7 * q + 7)
                if q == 0:
                    pe.wait_ge(s_ones, 1)
                T.matmul(bank[7][:], ones[:], sumsq[:], start=True, stop=True).then_inc(s_mean, 1)

            def ffn(f, hname):
                nb, at, dt, aa = N0[f"ffn{f}"], AT0[f"ffn{f}"], DT0[f"ffn{f}"], ACT0[f]

                def body(i, ada, first=False):
                    if not first:
                        pe.wait_ge(s_actT, at + 2 * i)
                    pair(nb, (0, 1), h_hi, h_lo, (s_hlo, H0[hname]) if first else None, i)
                    if not first:
                        pe.wait_ge(s_dveT, dt + 2 * i)
                    pair(nb + 2, (2, 3), h_hi, h_lo, None, i)
                    if ada:
                        pe.wait_ge(s_adastep, 8 * N_MOD * f + 8 + 8 * i)
                        if not (f == 0 and first):
                            pe.wait_ge(s_mod, N_MOD * f + i)
                        for j in range(4):
                            ins = T.matmul(bank[6][:, j:j + 1], ada_acc[:, j * P:(j + 1) * P], small[:, 66:67],
                                           start=True, stop=True)
                        ins.then_inc(s_adamm, 1)

                body(0, f < 4, True)
                if f < 4:
                    with pe.Fori(1, N_MOD) as i:
                        body(i, True)
                    with pe.Fori(N_MOD, NF // 2) as i:
                        body(i, False)
                else:
                    with pe.Fori(1, NF // 2) as i:
                        body(i, False)

                def down(half, kk, i=0, loop=False, signal=False):
                    n = nb + 44 + 11 * half + kk
                    hi, lo = slab(n, 512)
                    pe.wait_ge(s_lo, n + 1 + 2 * i)
                    if half == 0:
                        pe.wait_ge(s_alo, aa + 2 * kk + 2 + 4 * i)
                    for c in range(4):
                        for j in range(2):
                            k = 2 * kk + j
                            if loop:
                                mh, ml = act_hi[:, bass.ds(i * 4 + k, 1), :], act_lo[:, bass.ds(i * 4 + k, 1), :]
                            else:
                                mh, ml = act_hi[:, k:k + 1, :], act_lo[:, k:k + 1, :]
                            dst = bank[(4 if half == 0 else 0) + c][:].rearrange("p (o s) -> p o s", o=1)
                            ins = mm3(dst, hi[:, j, c * P:(c + 1) * P],
                                      lo[:, j, c * P:(c + 1) * P], mh, ml, kk == 0 and j == 0, signal and j == 1)
                        if signal and c < 3:
                            ins.then_inc(s_down, 1)
                    ins.then_inc(s_used, 1)

                for half in range(2):
                    down(half, 0)
                    with pe.Fori(0, 4) as i:
                        down(half, 1, i, True)
                        down(half, 2, i, True)
                    down(half, 9)
                    down(half, 10, signal=True)

            def out_phase(name, mh, ml, ready, free):
                nb, dt = N0[name], DT0[name]
                for s, v in free:
                    pe.wait_ge(s, v)
                for j in range(4):
                    if j >= 2:
                        pe.wait_ge(s_x, free_x[name] + 2 * (j - 1))
                    pair(nb + 2 * j, (2 * (j % 2), 2 * (j % 2) + 1), mh, ml, ready if j == 0 else None)

            free_x = {"pool_out": 8, "out0": 24, "out1": 56, "out2": 80}

            def project(m, groups, bufs, hname):
                nb, at = N0[f"proj{m}"], AT0[f"proj{m}"]
                n, post, tiles_done = nb, [0], 0
                turn = half_turn if m == 0 else part_turn
                pending = []
                counts = []

                def posts(tiles):
                    for kind, idx, tile in tiles:
                        if kind == "u":
                            continue
                        j = post[0]
                        post[0] += 1
                        src, aux = bufs["stage"][:, j % 4, :], bank[4 + j % 2]
                        pe.wait_ge(s_actT, at + tile + 1)
                        if j >= 2:
                            pe.wait_ge(s_post, PO0[m] + j - 1)
                        if kind in ("v", "va"):
                            for b in range(NB):
                                ins = T.transpose(aux[:, b * P:(b + 1) * P], src[:, b * P:(b + 1) * P], ident)
                        else:
                            ins = T.matmul(aux[:], turn, src, start=True, stop=True)
                        ins.then_inc(s_postmm, 1)

                for g, (slabs, tiles) in enumerate(groups):
                    if g >= 2:
                        pe.wait_ge(s_actT, at + counts[g - 2])
                    if slabs == 2:
                        pair(n, (2 * (g % 2), 2 * (g % 2) + 1), h_hi, h_lo, (s_hlo, H0[hname]) if g == 0 else None)
                    else:
                        hi, lo = slab(n, P)
                        pe.wait_ge(s_lo, n + 1)
                        for k in range(KC):
                            ins = mm3(bank[2 * (g % 2)][:], hi[:, k, :], lo[:, k, :], h_hi[:, k, :], h_lo[:, k, :],
                                      k == 0, k == KC - 1)
                        ins.then_inc(s_used, 1)
                    n += slabs
                    if m and g == 0:
                        pe.wait_ge(s_iwl, m)
                        for b in range(NB):
                            dst = bank[6][:, 4 * b:4 * b + 4]
                            for k in range(KC):
                                tok = slice(b * P, (b + 1) * P)
                                wh, wl = bufs["iwh"][:, k, :], bufs["iwl"][:, k, :]
                                T.matmul(dst, h_hi[:, k, tok], wh, start=k == 0, stop=False)
                                T.matmul(dst, h_hi[:, k, tok], wl, start=False, stop=False)
                                ins = T.matmul(dst, h_lo[:, k, tok], wh, start=False, stop=k == KC - 1)
                        ins.then_inc(s_iw, 1)
                    posts(pending)
                    if m and g == 1:
                        for w in range(4):
                            ins = T.transpose(bank[7][:, w * P:(w + 1) * P], bufs["sguw"][:, w, :], ident)
                        ins.then_inc(s_wtr, 1)
                    pending = [(k, i, tiles_done + j) for j, (k, i) in enumerate(tiles)]
                    tiles_done += len(tiles)
                    counts.append(tiles_done)
                    if m and 3 <= g <= 5:
                        b = g - 2
                        if g == 3:
                            pe.wait_ge(s_post, PO0[m] + 3)
                            pe.wait_ge(s_wi, m)
                            pe.wait_ge(s_wT, m)
                        for h in range(IDX_HEADS):
                            x = 4 * (g - 3) + h
                            y = 12 * (m - 1) + x
                            if x >= 2:
                                pe.wait_ge(s_relu, y - 1)
                            r = slice(HD * (h % 2), HD * (h % 2) + HD)
                            T.matmul(bank[6 + x % 2][:, 0:(b + 1) * P], bufs["iqT"][r, h // 2, b * P:(b + 1) * P],
                                     bufs["ikT"][r, 0, 0:(b + 1) * P], start=True, stop=True).then_inc(s_idxmm, 1)
                posts(pending)
                if m:
                    pe.wait_ge(s_post, PO0[m] + 19)
                    pe.wait_ge(s_relu, 12 * m)
                    for g in range(SGU_GROUPS):
                        if g >= 2:
                            pe.wait_ge(s_sgu, 4 * (m - 1) + g - 1)
                        for b in range(NB):
                            ins = T.matmul(bank[6 + g % 2][:, b * P:(b + 1) * P], bufs["vaN"][:, b, g * P:(g + 1) * P],
                                           bufs["wT"][:, g, :], start=True, stop=True)
                        ins.then_inc(s_sgumm, 1)

            def attention(m):
                t = ATT[m]
                u0, hp0, bufs, nu, nh = t["u0"], t["hp0"], t["b"], t["nu"], t["nh"]
                n_post = 24 if m == 0 else 19
                pe.wait_ge(s_post, PO0[m] + n_post)
                pe.wait_ge(s_actT, AT0[f"out{m}"])

                def scores(u):
                    h, b = u // 4, u % 4
                    if u >= 2:
                        pe.wait_ge(s_exp, u0 + u - 1)
                    r = slice(HD * (h % 2), HD * (h % 2) + HD)
                    T.matmul(bank[u % 2][:, 0:(b + 1) * P], bufs["qT"][r, h // 2, b * P:(b + 1) * P],
                             bufs["kT"][r, h // 2, 0:(b + 1) * P], start=True, stop=True).then_inc(s_scmm, 1)

                def values(u):
                    h, b = u // 4, u % 4
                    pe.wait_ge(s_pt, u0 + u + 1)
                    if u % 8 == 0 and u >= 16:
                        pe.wait_ge(s_o, hp0 + u // 8 - 1)
                    slot = ((h % 2) * 4 + b) * HD
                    for k in range(b + 1):
                        ins = T.matmul(bank[4 + (u // 8) % 2][:, slot:slot + HD], bufs["PT"][:, u % 2, k * P:(k + 1) * P],
                                       bufs["vN"][:, k, h * HD:(h + 1) * HD], start=k == 0, stop=k == b)
                    ins.then_inc(s_pv, 1)

                scores(0)
                scores(1)
                for u in range(nu):
                    b = u % 4
                    pe.wait_ge(s_exp, u0 + u + 1)
                    if u >= 2:
                        pe.wait_ge(s_pt, u0 + u - 1)
                    for k in range(b + 1):
                        ins = T.transpose(bank[2 + u % 2][:, k * P:(k + 1) * P], bufs["P"][:, u % 2, k * P:(k + 1) * P], ident)
                    ins.then_inc(s_tr, 1)
                    if u + 2 < nu:
                        scores(u + 2)
                    if u:
                        values(u - 1)
                values(nu - 1)
                c0 = 0 if m == 0 else 4
                pe.wait_ge(s_on, 4 * m + 4)
                if m:
                    pe.wait_ge(s_sgu, 4 * m)
                for c in range(c0, KC):
                    o = OT0[m] + c - c0
                    if c - c0 >= 2:
                        pe.wait_ge(s_hlo, H0[f"attn{m}"] + c - 1)
                    col = (c - c0) * P
                    for b in range(NB):
                        ins = T.transpose(bank[6 + c % 2][:, b * P:(b + 1) * P], bufs["oN"][:, b, col:col + P], ident)
                    ins.then_inc(s_otr, 1)

            pe.wait_ge(s_const, 32)
            pe.wait_ge(s_vecs, 16 * 11)
            T.transpose(bank[4][:, 0:N_VEC], vrows[0:N_VEC, :], ident[0:N_VEC, 0:N_VEC])
            n = N_MOD * KC
            for l in range(2):
                ins = T.transpose(bank[5][:, n * l:n * l + n], brows[0:n, l, :], ident[0:n, 0:n])
            ins.then_inc(s_setup, 1)
            for k in range(KC):
                if k == 0:
                    for b in range(NB):
                        pe.wait_ge(s_xin[b], 16)
                if k >= 4:
                    pe.wait_ge(s_x, k - 3)
                for b in range(NB):
                    ins = T.transpose(bank[k % 4][:, b * P:(b + 1) * P], x_nat[:, b, k * P:(k + 1) * P], ident)
                ins.then_inc(s_xtr, 1)
            mean(0)
            nb = N0["pool_in"]
            pe.wait_ge(s_x, 8)
            for j in range(4):
                if j >= 2:
                    pe.wait_ge(s_actT, 2 * (j - 1))
                pair(nb + 2 * j, (2 * (j % 2), 2 * (j % 2) + 1), h_hi, h_lo, (s_hlo, H0["n0"]) if j == 0 else None)
            nb = N0["group"]
            pe.wait_ge(s_actT, 8)
            for j in range(2):
                pe.wait_ge(s_lo, nb + j + 1)
                hi, lo = slab(nb + j, 256)
                for g in range(2):
                    for c in range(2):
                        t = 4 * j + 2 * g + c
                        for k in range(2):
                            src = 4 * j + 2 * g + k
                            pe.wait_ge(s_hlo, H0["pool"] + src + 1)
                            ins = mm3(bank[t][:], hi[:, 2 * g + k, c * P:(c + 1) * P], lo[:, 2 * g + k, c * P:(c + 1) * P],
                                      h_hi[:, src, :], h_lo[:, src, :], k == 0, k == 1)
                ins.then_inc(s_used, 1)
            out_phase("pool_out", act_hi, act_lo, (s_alo, 0), [(s_alo, 4)])
            mean(1)
            ffn(0, "n1")
            mean(2)
            project(0, A1_GROUPS, a1, "n2")
            attention(0)
            out_phase("out0", h_hi, h_lo, (s_hlo, H0["attn0"]), [(s_pt, ATT[1]["u0"]), (s_exp, ATT[1]["u0"])])
            mean(3)
            ffn(1, "n3")
            mean(4)
            mean(5)
            for l in range(2):
                q = 5 + 3 * l
                ffn(2 + 2 * l, ["n5", "n8"][l])
                mean(q + 1)
                project(1 + l, A2_GROUPS, a2, ["n6", "n9"][l])
                attention(1 + l)
                end = ATT[1 + l]["u0"] + ATT[1 + l]["nu"]
                out_phase(f"out{1 + l}", h_hi, h_lo, (s_hlo, H0[f"attn{1 + l}"]), [(s_pt, end), (s_exp, end)])
                mean(q + 2)
                ffn(3 + 2 * l, ["n7", "n10"][l])
                mean(q + 3)
            for b in range(NB):
                for half in range(2):
                    n = 2 * b + half
                    if n == 0:
                        pe.wait_ge(s_x, 8 * 13)
                    if n >= 4:
                        pe.wait_ge(s_ynat, n - 3)
                    for k in range(4):
                        ins = T.transpose(bank[n % 4][:, k * P:(k + 1) * P], yT[:, 4 * half + k, b * P:(b + 1) * P], ident)
                    ins.then_inc(s_ytr, 1)


_INS = ['x', 'norm_mix', 'norm_ffn', 'norm_final', 'pool_w_in', 'pool_w_group', 'pool_scale', 'pool_w_out',
        'attn_w_qkv', 'attn_w_out', 'ffn_w_gate', 'ffn_w_up', 'ffn_w_down', 'c_2', 'positions_2', 'ada_w_2',
        'ada_b_2', 'norm_ffn1_2', 'ffn1_w_in_2', 'ffn1_w_out_2', 'norm_mix_2', 'mix_w_in_2', 'sgu_w_2', 'sgu_b_2',
        'mix_w_out_2', 'norm_ffn2_2', 'ffn2_w_in_2', 'ffn2_w_out_2', 'final_norm_2']
_CONSTS = ['squares', 'rope', 'masks', 'small']


def kernel(**inputs):
    import numpy as _np
    import concourse.bacc as _bacc
    from concourse import mybir as _mybir
    from concourse.bass_utils import run_bass_kernel_spmd as _run

    nc = _bacc.Bacc("TRN2", target_bir_lowering=False, num_devices=1)
    arrays, args = {}, []
    consts = dict(zip(_CONSTS, constants()))
    for name in _INS + _CONSTS:
        a = _np.ascontiguousarray(inputs[name] if name in inputs else consts[name])
        arrays[f"in_{name}_dram"] = a
        args.append(nc.dram_tensor(f"in_{name}_dram", a.shape, _mybir.dt.from_np(a.dtype), kind="ExternalInput").ap())
    out = nc.dram_tensor("out_0_dram", (1, S, D), F32, kind="ExternalOutput").ap()
    program(nc, *args, out)
    r = _run(nc, [arrays], core_ids=[0])
    return r.results[0]["out_0_dram"]
```

```python
from contextlib import ExitStack

import numpy as np

import concourse.bass as bass
from concourse import mybir

P = 128
S = 512
D = 1024
KC = D // P
NB = S // P
DFF = 2816
NF = DFF // P
HD = 64
EPS = 1e-6
NEG = -1e30
TAKEN = -3e38
SLAB = 1024
RAW = 4
SPL = 2

F32 = mybir.dt.float32
FR = mybir.dt.float32r
I32 = mybir.dt.int32
ACT = mybir.ActivationFunctionType
ALU = mybir.AluOpType
AX_X = mybir.AxisListType.X

POOL_WINDOWS = (2, 4, 8, 16)
HEAD_GROUPS = ((0, 6), (6, 11), (11, 16))
TOPK = 128
SGU_GROUPS = 4
IDX_HEADS = 4
N_MOD = 9
OFF_U, OFF_VA, OFF_Q, OFF_K, OFF_V, OFF_IQ, OFF_IK, OFF_IW = 0, 512, 1024, 1536, 2048, 2560, 2816, 2880

VEC_ROWS = {}
_at = 0
for _name, _n in (("norm_mix", 16), ("norm_ffn", 16), ("norm_final", 8), ("pool_scale", 8), ("c", 8),
                  ("f1", 16), ("mix2", 16), ("f2", 16), ("final2", 8)):
    VEC_ROWS[_name] = _at
    _at += _n
N_VEC = _at

TRI = [64 * b * (b + 1) for b in range(NB + 1)]
PT_BLOCKS = 3 * (NB - 1) + NB


def constants():
    ident = np.eye(P, dtype=np.float32)
    half_turn = np.zeros((P, P), np.float32)
    part_turn = np.zeros((P, P), np.float32)
    for h in (0, HD):
        for d in range(HD // 2):
            half_turn[h + d + HD // 2, h + d] = -1.0
            half_turn[h + d, h + d + HD // 2] = 1.0
        for d in range(HD // 8):
            part_turn[h + d + HD // 8, h + d] = -1.0
            part_turn[h + d, h + d + HD // 8] = 1.0
    upper = np.triu(np.ones((P, P), np.float32))
    squares = np.concatenate([ident, half_turn, part_turn, upper], 1)

    f1 = (1.0 / (np.float32(10000.0) ** (np.arange(0, HD, 2, dtype=np.float32) / np.float32(HD)))).astype(np.float32)
    ang = (np.arange(S, dtype=np.float32)[None, :] * f1[:, None]).astype(np.float32)
    ang = np.tile(ang, (4, 1)).astype(np.float64)
    rope = np.concatenate([np.cos(ang), np.sin(ang)], 1).astype(np.float32)

    q = np.arange(S)[:, None]
    k = np.arange(S)[None, :]
    rules = [(q >= k) & (q - k <= 128), (q >= k) & ((q - k) % 4 == 0), (q >= k) & ((q - k) % 16 == 0), q >= k]
    masks = np.zeros((4, P, TRI[NB]), np.float32)
    for n, rule in enumerate(rules):
        bias = np.where(rule, 0.0, NEG).astype(np.float32)
        for b in range(NB):
            masks[n, :, TRI[b]:TRI[b + 1]] = bias[b * P:(b + 1) * P, :(b + 1) * P]

    t = np.arange(16)
    ratio = np.stack([w / np.minimum(t + 1, w) for w in POOL_WINDOWS]).astype(np.float32)
    small = np.zeros((P, 67), np.float32)
    small[:, :64] = ratio.reshape(1, 64)
    rot = HD // 4
    f2 = np.float32(500000.0) ** (-np.arange(0, rot, 2, dtype=np.float32) / np.float32(rot))
    for h in (0, HD):
        small[h:h + rot // 2, 64] = f2
        small[h + rot // 2:h + rot, 64] = f2
    small[:, 65] = EPS
    small[:, 66] = 1.0
    return squares, rope, masks, small


def two_pi_parts():
    left, parts = 2.0 * np.pi, []
    for bits in (9, 9, 9):
        e = np.floor(np.log2(left))
        step = 2.0 ** (e - bits + 1)
        c = np.floor(left / step) * step
        parts.append(float(c))
        left -= c
    parts.append(float(np.float32(left)))
    return parts


def program(nc, x, norm_mix, norm_ffn, norm_final, pool_w_in, pool_w_group, pool_scale, pool_w_out,
            attn_w_qkv, attn_w_out, ffn_w_gate, ffn_w_up, ffn_w_down, c_2, positions_2, ada_w_2, ada_b_2,
            norm_ffn1_2, ffn1_w_in_2, ffn1_w_out_2, norm_mix_2, mix_w_in_2, sgu_w_2, sgu_b_2, mix_w_out_2,
            norm_ffn2_2, ffn2_w_in_2, ffn2_w_out_2, final_norm_2, squares_c, rope_c, masks_c, small_c, out):
    with ExitStack() as ctx:
        arena_at = (nc.sbuf_base + 31) // 32 * 32
        ctx.enter_context(nc.sbuf_tensor("arena", [P, 212480 // 4], F32))
        cursor = [arena_at]

        def place(name, shape, dt=F32, at=None):
            size = int(np.prod(shape[1:])) * 4
            if at is None:
                at = cursor[0]
                cursor[0] += (size + 31) // 32 * 32
                assert cursor[0] <= arena_at + 212480, (name, cursor[0] - arena_at)
            return nc.alloc_sbuf_tensor_at(name, shape, dt, offset=at)

        xT = place("xT", [P, KC, S])
        h_hi = place("h_hi", [P, KC, S], FR)
        h_lo = place("h_lo", [P, KC, S], FR)
        raw = place("raw", [P, RAW, SLAB])
        w_hi = place("w_hi", [P, SPL, SLAB], FR)
        w_lo = place("w_lo", [P, SPL, SLAB], FR)
        ada_at = cursor[0]
        ada_w = place("ada_w", [P, 2, 4, 512])
        ada_acc = place("ada_acc", [P, 512])
        sumsq = place("sumsq", [P, S])
        sq_at = cursor[0]
        sq = place("sq", [P, 2, S])
        diag_hi = place("diag_hi", [P, NB, P], FR, at=sq_at)
        diag_lo = place("diag_lo", [P, NB, P], FR, at=sq_at + S * 4)
        turn_hi = place("turn_hi", [P, 2, P], FR)
        ones_r = place("ones_r", [P, P], FR)
        sd4 = place("sd4", [P, 4, NB])
        work_at = cursor[0]
        work = place("work", [P, 4, S])
        vec = place("vec", [P, N_VEC])
        adab = place("adab", [P, 2 * N_MOD * KC])
        mod = place("mod", [P, 2 * N_MOD * KC])
        coefs = place("coefs", [P, 2, 5, KC])
        squares = place("squares", [P, 4, P])
        small = place("small", [P, 67])
        ones = place("ones", [P, 1])
        cact = place("cact", [P, KC])
        scratch1 = place("scratch1", [P, 1])
        reg = cursor[0]
        REG_END = reg + 2 * NF * S * 4
        assert REG_END <= arena_at + 212480, REG_END - arena_at
        ident, upper = squares[:, 0, :], squares[:, 3, :]

        act_hi = place("act_hi", [P, NF, S], FR, at=reg)
        act_lo = place("act_lo", [P, NF, S], FR, at=reg + NF * S * 4)

        def layout(prefix, items):
            at, got = reg, {}
            for name, shape, dt in items:
                got[name] = place(prefix + name, shape, dt, at=at)
                at += (int(np.prod(shape[1:])) * (2 if dt == mybir.dt.bfloat16 else 4) + 31) // 32 * 32
            assert at <= REG_END, (prefix, at - REG_END)
            return got

        x_nat = place("x_nat", [P, NB, D], at=reg + 8 * S * 4)
        vrows = place("vrows", [P, P], at=reg + 16 * S * 4)
        brows = place("brows", [P, 2, P], at=reg + 16 * S * 4 + 512)
        uP = place("uP", [P, 8, S], at=ada_at)
        p_hi = place("p_hi", [P, 8, S], FR, at=reg + 8 * S * 4)
        p_lo = place("p_lo", [P, 8, S], FR, at=reg + 8 * S * 4 + NF * S * 4)
        winA = place("winA", [P, 2, S], at=reg + 17 * S * 4)
        pP = place("pP", [P, 2, S], at=reg + 19 * S * 4)

        BF = mybir.dt.bfloat16
        side = {"st_hi": place("st_hi", [P, 2, S], FR, at=ada_at), "st_lo": place("st_lo", [P, 2, S], FR, at=ada_at + 2 * S * 4),
                "st_v": place("st_v", [P, 2, S], at=ada_at), "ang": place("ang", [P, 4, S], at=ada_at),
                "rot": place("rot", [P, 2, S], at=ada_at + 4 * S * 4), "turned": place("turned", [P, S], at=ada_at + 6 * S * 4),
                "cos": place("cos", [P, 2, S], at=ada_at + 7 * S * 4),
                "P": place("probs", [P, 2, S], at=ada_at),
                "PTh": place("probsT_hi", [P, 2, PT_BLOCKS * P], FR, at=ada_at + 2 * S * 4),
                "PTl0": place("probsT_lo0", [P, PT_BLOCKS * P], FR, at=ada_at + 2 * S * 4 + 2 * PT_BLOCKS * P * 4)}
        assert 2 * S * 4 + 3 * PT_BLOCKS * P * 4 <= 12 * S * 4
        sel = place("sel", [P, 16, HD], FR, at=work_at + 2 * S * 4)

        def head_layout(prefix, n, more):
            got = layout(prefix, [("qTh", [P, n, S], FR), ("qTl", [P, n, S], FR), ("kTh", [P, n, S], FR),
                                  ("kTl", [P, n, S], FR), ("vN", [P, NB, n * P], F32)] + more)
            got["oT"] = place(prefix + "oT", [P, n, S], at=reg)
            got["fine"] = place(prefix + "fine", [P, 6, NB, 16], at=reg + 2 * n * S * 4)
            got["cTh"] = place(prefix + "cTh", [P, S], FR, at=reg + 3 * n * S * 4)
            got["cTl"] = place(prefix + "cTl", [P, S], FR, at=reg + (3 * n + 1) * S * 4)
            got["PTl1"] = place(prefix + "probsT_lo1", [P, PT_BLOCKS * P], FR,
                                at=reg + 4 * n * S * 4 + (0 if n == 8 else 4 * S * 4))
            return got | side

        a1 = head_layout("a1_", 8, [("masks", [P, 3, TRI[NB]], BF), ("nmx", [P, 64], F32), ("den", [P, 64], F32)])
        a2 = head_layout("a2_", 4, [
            ("iqTh", [P, 2, S], FR), ("iqTl", [P, 2, S], FR), ("ikTh", [P, 1, S], FR), ("ikTl", [P, 1, S], FR),
            ("uT", [P, 4, S], F32), ("vaN", [P, NB, 512], F32),
            ("score", [P, TRI[NB]], F32), ("causal", [P, TRI[NB]], BF), ("masks", [P, 1, TRI[NB]], BF),
            ("sguw", [P, 4, P], F32), ("wT", [P, 4, P], F32), ("bbc", [P, 4, P], F32),
            ("nmx", [P, 32], F32), ("den", [P, 32], F32), ("wi", [P, NB, 4], F32),
            ("m8", [P, 3, 8], F32)])
        yT = place("yT", [P, KC, S], at=reg)
        y_nat = place("y_nat", [P, NB, D], at=reg + KC * S * 4)

        bank = [ctx.enter_context(nc.psum_tensor(f"bank{i}", [P, S], F32)) for i in range(8)]

        def sem(name):
            return ctx.enter_context(nc.semaphore(name))

        s_const = sem("consts_loaded")
        s_vecs = sem("vectors_loaded")
        s_xin = [sem(f"x_block{b}_loaded") for b in range(NB)]
        s_load = [sem(f"slab_loaded_slot{j}") for j in range(RAW)]
        s_ik2 = sem("index_weights_loaded")
        s_hi = sem("slab_hi_ready")
        s_lo = sem("slab_lo_ready")
        s_used = sem("slab_used_by_pe")
        s_x = sem("x_chunk_ready")
        s_sq = sem("square_ready")
        s_sum = sem("square_added")
        s_mean = sem("mean_ready")
        s_sd = sem("deviation_ready")
        s_rstd = sem("rstd_diagonal_ready")
        s_spread = sem("rstd_on_all_partitions")
        s_htmp = sem("normed_chunk_ready")
        s_hhi = sem("h_hi_ready")
        s_hlo = sem("h_lo_ready")
        s_actT = sem("tile_out_by_act")
        s_dveT = sem("tile_out_by_dve")
        s_down = sem("down_chunk_done")
        s_ahi = sem("act_hi_ready")
        s_alo = sem("act_lo_ready")
        s_adaload = [sem(f"ada_half{h}_loaded") for h in range(2)]
        s_adastep = sem("ada_partial_sum")
        s_adamm = sem("ada_reduced")
        s_mod = sem("modulation_ready")
        s_dve = sem("dve_step_done")
        s_act = sem("act_step_done")
        s_setup = sem("vectors_transposed")
        s_vec = sem("vectors_on_partitions")
        s_ones = sem("ones_ready")
        s_xtr = sem("x_transposed")
        s_win = sem("window_ready")
        s_phi = sem("pooled_hi_ready")
        s_plo = sem("pooled_lo_ready")
        s_phaseld = sem("mix_tables_loaded")
        s_pos = sem("positions_loaded")
        s_dveT2 = sem("staged_tile_out_by_dve")
        s_rot = sem("rotated_tile_ready")
        s_roth = sem("rotated_hi_ready")
        s_postmm = sem("post_mm_done")
        s_post = sem("post_done")
        s_iw = sem("index_weights_mm")
        s_wi = sem("index_weights_ready")
        s_iwT = sem("index_weights_staged")
        s_tab = sem("rope_angle_ready")
        s_sin = sem("rope_table_ready")
        s_wtr = sem("sgu_w_transposed")
        s_wT = sem("sgu_w_ready")
        s_idxmm = sem("index_scores_mm")
        s_relu = sem("index_relu_ready")
        s_idx = sem("index_score_added")
        s_mask = sem("topk_mask_ready")
        s_sgumm = sem("sgu_mm_done")
        s_sgu = sem("sgu_out_ready")
        s_scmm = sem("scores_mm")
        s_masked = sem("scores_masked")
        s_exp = sem("exp_done")
        s_tr = sem("probs_transposed")
        s_pth = sem("probsT_hi_ready")
        s_pt = sem("probsT_ready")
        s_vh = sem("v_hi_ready")
        s_vl = sem("v_lo_ready")
        s_sel = sem("head_selection_ready")
        s_ch = sem("coef_hi_ready")
        s_cl = sem("coef_lo_ready")
        s_pv = sem("pv_done")
        s_o = sem("o_out")
        s_aw = sem("alpha_exponent_ready")
        s_ae = sem("alpha_exp_done")
        s_on = sem("o_scaled")
        s_otr = sem("coef_spread")
        s_ytr = sem("y_transposed")
        s_ynat = sem("y_natural_ready")
        s_out = [sem(f"out_block{b}_stored") for b in range(NB)]

        def kview(w):
            return w.rearrange("(k p) c -> p k c", p=P)

        def pairs_of(w, col0, n_pairs):
            v = kview(w)
            return [v[:, 4 * half:4 * half + 4, col0 + 256 * j:col0 + 256 * j + 256]
                    for j in range(n_pairs) for half in range(2)]

        def down_slabs(w):
            v = kview(w)
            return [v[:, 2 * kk:2 * kk + 2, 512 * half:512 * half + 512] for half in range(2) for kk in range(NF // 2)]

        ROTATED = ("q", "k", "iq", "ik")
        A1_GROUPS = [(2, [(kind, 2 * j), (kind, 2 * j + 1)]) for kind in ("q", "k", "v") for j in range(4)]
        A2_GROUPS = [(2, [("iq", 0), ("iq", 1)]), (1, [("ik", 0)])]
        for kind in ("q", "k", "v", "va", "u"):
            A2_GROUPS += [(2, [(kind, 2 * j), (kind, 2 * j + 1)]) for j in range(2)]

        wg = pool_w_group[0].rearrange("g (k p) e -> p (g k) e", p=P)
        n_slabs = 0
        N0 = {}
        for name, n in [("pool_in", 8), ("group", 2), ("pool_out", 8), ("ffn0", 66), ("proj0", 24), ("out0", 8),
                        ("ffn1", 66), ("ffn2", 66), ("proj1", 23), ("out1", 8), ("ffn3", 66), ("ffn4", 66),
                        ("proj2", 23), ("out2", 8), ("ffn5", 66)]:
            N0[name] = n_slabs
            n_slabs += n

        gate_of = [ffn_w_gate[0], ffn_w_gate[1]] + [None] * 4
        up_of = [ffn_w_up[0], ffn_w_up[1]] + [None] * 4
        down_of = [ffn_w_down[0], ffn_w_down[1], ffn1_w_out_2[0], ffn2_w_out_2[0], ffn1_w_out_2[1], ffn2_w_out_2[1]]
        for f, w in ((2, ffn1_w_in_2[0]), (3, ffn2_w_in_2[0]), (4, ffn1_w_in_2[1]), (5, ffn2_w_in_2[1])):
            gate_of[f], up_of[f] = w[:, 0:DFF], w[:, DFF:2 * DFF]

        H0 = {name: 8 * i for i, name in enumerate(
            ["n0", "n1", "n2", "attn0", "n3", "n5", "n6", "attn1", "n7", "n8", "n9", "attn2", "n10"])}
        HT0 = {name: 8 * i for i, name in enumerate(["n0", "n1", "n2", "n3", "n5", "n6", "n7", "n8", "n9", "n10"])}
        LATE = {1: "ffn0", 2: "proj0", 3: "ffn1", 4: "ffn2", 6: "proj1", 7: "ffn3", 8: "ffn4", 9: "proj2", 10: "ffn5"}
        OT0 = [0, 9, 14]
        OUT_BANK = {"pool_out": 4, "out0": 0, "out1": 0, "out2": 0}
        SCORE_BANKS = (0, 1, 6)
        V0 = [0, 8, 12]
        ACT0 = {"pool": 0} | {f: 8 + NF * f for f in range(6)}
        ATT = [dict(nh=16, u0=0, h0=0, b=a1), dict(nh=8, u0=64, h0=16, b=a2), dict(nh=8, u0=96, h0=24, b=a2)]
        for t in ATT:
            t["nu"] = 4 * t["nh"]
        AT0, DT0, a, d = {}, {}, 0, 0
        for name in N0:
            AT0[name], DT0[name] = a, d
            if name == "pool_in":
                a += 8
            elif name.startswith("ffn"):
                a += NF
                d += NF
            elif name.startswith("proj"):
                a += sum(len(t) for _, t in (A1_GROUPS if name == "proj0" else A2_GROUPS))
        PO0 = [0, 24, 24 + 19]
        RO0 = [0, 16, 16 + 11]

        block = ctx.enter_context(nc.Block())

        @block.sync
        def _(sp):
            def load(nb, src, i=0, shape=None):
                if nb >= RAW:
                    sp.wait_ge(s_lo, nb - RAW + 1 + 4 * i)
                dst = raw[:, nb % RAW, :].rearrange("p (k c) -> p k c", c=shape)
                return sp.dma_start(dst, src).then_inc(s_load[nb % RAW], 16)

            for b in range(NB):
                sp.dma_start(x_nat[:, b, :], x[0, b * P:(b + 1) * P, :]).then_inc(s_xin[b], 16)

            def load_list(name, srcs, c):
                for j, src in enumerate(srcs):
                    load(N0[name] + j, src, shape=c)

            def load_ffn(f):
                nb = N0[f"ffn{f}"]
                g, u = kview(gate_of[f]), kview(up_of[f])
                with sp.Fori(0, NF // 2) as i:
                    for j, w in enumerate((g, g, u, u)):
                        half = j % 2
                        load(nb + j, w[:, 4 * half:4 * half + 4, bass.ds(i * 256, 256)], i, shape=256)
                for j, src in enumerate(down_slabs(down_of[f])):
                    load(nb + 44 + j, src, shape=512)

            by_pair = pairs_of(pool_w_in[0], 0, 4)
            load_list("pool_in", by_pair[6:8] + by_pair[4:6] + by_pair[2:4] + by_pair[0:2], 256)
            load_list("group", [wg[:, 4 * j:4 * j + 4, :] for j in (1, 0)], 256)
            halves = pairs_of(pool_w_out[0], 0, 4)
            load_list("pool_out", [halves[j ^ 1] for j in range(8)], 256)
            load_ffn(0)
            load_list("proj0", pairs_of(attn_w_qkv[0], 0, 12), 256)
            load_list("out0", pairs_of(attn_w_out[0], 0, 4), 256)
            load_ffn(1)
            for layer in range(2):
                load_ffn(2 + 2 * layer)
                w = mix_w_in_2[layer]
                name = f"proj{1 + layer}"
                nb = N0[name]
                for j, src in enumerate(pairs_of(w, OFF_IQ, 1)):
                    load(nb + j, src, shape=256)
                nk = nb + 2
                sp.wait_ge(s_lo, nk - RAW + 1)
                dst = raw[:, nk % RAW, :].rearrange("p (k c) -> p k c", c=P)
                ikw = kview(w)[:, :, OFF_IK:OFF_IK + HD]
                sp.dma_start(dst[:, :, 0:HD], ikw).then_inc(s_load[nk % RAW], 16)
                sp.dma_start(dst[:, :, HD:HD + IDX_HEADS], kview(w)[:, :, OFF_IW:OFF_IW + IDX_HEADS]).then_inc(s_ik2, 16)
                sp.dma_start(dst[:, :, HD + IDX_HEADS:P], ikw[:, :, IDX_HEADS:HD]).then_inc(s_ik2, 16)
                rest = []
                for off in (OFF_Q, OFF_K, OFF_V, OFF_VA, OFF_U):
                    rest += pairs_of(w, off, 2)
                for j, src in enumerate(rest):
                    load(nb + 3 + j, src, shape=256)
                load_list(f"out{1 + layer}", pairs_of(mix_w_out_2[layer], 0, 4), 256)
                load_ffn(3 + 2 * layer)
            for b in range(NB):
                sp.wait_ge(s_ynat, 2 * b + 2)
                sp.dma_start(out[0, b * P:(b + 1) * P, :], y_nat[:, b, :]).then_inc(s_out[b], 16)
            for b in range(NB):
                sp.wait_ge(s_out[b], 16)

        @block.gpsimd
        def _(pool):
            def ada_loads(f):
                w = kview(ada_w_2[f // 2])

                def halves(i, first=False):
                    for half in range(2):
                        if not first:
                            pool.wait_ge(s_adastep, 8 * (N_MOD * f - 1) + 4 * half + 4 + 8 * i)
                        pool.dma_start(ada_w[:, half], w[:, 4 * half:4 * half + 4, bass.ds(i * 512 + (f % 2) * N_MOD * 512, 512)])\
                            .then_inc(s_adaload[half], 16)

                if f == 0:
                    halves(0, True)
                with pool.Fori(1 if f == 0 else 0, N_MOD) as i:
                    halves(i)

            def mix_tables(m):
                pool.wait_ge(s_used, N0[f"proj{m}"])
                if m == 0:
                    pool.wait_ge(s_adastep, 8 * N_MOD)
                    pool.dma_start(a1["cos"][:], rope_c.rearrange("p (n s) -> p n s", s=S)).then_inc(s_phaseld, 16)
                    for g in range(3):
                        pool.dma_start(a1["masks"][:, g, :], masks_c[g]).then_inc(s_phaseld, 16)
                    return
                l = m - 1
                pool.dma_start(a2["causal"][:], masks_c[3]).then_inc(s_phaseld, 16)
                pool.dma_start(a2["masks"][:, 0, 0:P], masks_c[3, :, 0:P]).then_inc(s_phaseld, 16)
                pool.dma_start(a2["sguw"][:], sgu_w_2[l].rearrange("g t s -> t g s")).then_inc(s_phaseld, 16)
                pool.dma_start(a2["bbc"][:].rearrange("p g t -> p (g t)"),
                               sgu_b_2[l].rearrange("g t -> (g t)")[None, :].to_broadcast([P, 4 * P]))\
                    .then_inc(s_phaseld, 16)

            def positions(m):
                pool.wait_ge(s_adastep, 8 * N_MOD * (m + 2))
                pool.dma_start(side["ang"][:, 3, :].bitcast(I32), positions_2[0:1, :].to_broadcast([P, S])).then_inc(s_pos, 16)

            pool.wait_ge(s_win, 8)
            ada_loads(0)
            mix_tables(0)
            pool.wait_ge(s_pv, ATT[1]["h0"])
            ada_loads(1)
            ada_loads(2)
            positions(1)
            mix_tables(1)
            pool.wait_ge(s_pv, ATT[2]["h0"])
            ada_loads(3)
            positions(2)
            mix_tables(2)

        PHASE_LD = [64, 64 + 64, 64 + 128]

        @block.scalar
        def _(act):
            steps = [0]

            def link(ins):
                steps[0] += 1
                ins.then_inc(s_act, 1)
                act.wait_ge(s_act, steps[0])

            def split_hi(nb, i=0):
                if nb >= n_slabs:
                    return
                act.wait_ge(s_load[nb % RAW], 16 * (nb // RAW + 1) + 16 * i)
                for m in (1, 2):
                    if nb == N0[f"proj{m}"] + 2:
                        act.wait_ge(s_ik2, 32 * m)
                if nb >= SPL:
                    act.wait_ge(s_used, nb - SPL + 1 + 4 * i)
                nc.scalar.activation(w_hi[:, nb % SPL, :], raw[:, nb % RAW, :], ACT.Copy).then_inc(s_hi, 1)

            def square_chunk(q, k):
                act.wait_ge(s_x, 8 * q + k + 1)
                n = 7 * q + k
                if k == 0:
                    if q:
                        act.wait_ge(s_sd, q)
                    nc.scalar.activation(sumsq[:], xT[:, 0, :], ACT.Square).then_inc(s_sq, 1)
                else:
                    if n - 1 >= 2:
                        act.wait_ge(s_sum, n - 2)
                    nc.scalar.activation(sq[:, (n - 1) % 2, :], xT[:, k, :], ACT.Square).then_inc(s_sq, 1)

            def norm_tail(q, hname, shift):
                nc.scalar.activation(scratch1[:], small[:, 65:66], ACT.Sqrt)
                act.wait_ge(s_mean, q + 1)
                nc.scalar.activation(sd4[:, 0, :], bank[7][:, 0:NB], ACT.Sqrt, bias=small[:, 65:66]).then_inc(s_sd, 1)
                if q in LATE:
                    split_hi(N0[LATE[q]] + 1)
                if hname is None:
                    return
                base = H0[hname]
                for k in range(KC):
                    act.wait_ge(s_htmp, HT0[hname] + k + 1)
                    if shift is None:
                        nc.scalar.activation(h_hi[:, k, :], work[:, k % 4, :], ACT.Copy).then_inc(s_hhi, 1)
                    else:
                        if k == 0:
                            act.wait_ge(s_mod, 18 if shift < 72 else 36)
                        nc.scalar.activation(h_hi[:, k, :], work[:, k % 4, :], ACT.Identity,
                                             bias=mod[:, shift + k:shift + k + 1]).then_inc(s_hhi, 1)

            def residual_squares(q, ks):
                for k in ks:
                    square_chunk(q, k)

            def ffn(f, q_next):
                nb, at, dt, aa = N0[f"ffn{f}"], AT0[f"ffn{f}"], DT0[f"ffn{f}"], ACT0[f]
                with act.Fori(0, NF // 2) as i:
                    split_hi(nb + 2, i)
                    split_hi(nb + 3, i)
                    for c in range(2):
                        act.wait_ge(s_used, nb + 2 + 4 * i)
                        nc.scalar.activation(work[:, c, :], bank[c][:], ACT.Silu).then_inc(s_actT, 1)
                    split_hi(nb + 4, i)
                    split_hi(nb + 5, i)
                    for c in range(2):
                        act.wait_ge(s_dveT, dt + c + 1 + 2 * i)
                        nc.scalar.activation(act_hi[:, bass.ds(i * 2 + c, 1), :], work[:, 2 + c:3 + c, :], ACT.Copy).then_inc(s_ahi, 1)
                for s in range(22):
                    if s < 21:
                        split_hi(nb + 44 + s + 2)
                    if f in (2, 4) and s in (17, 19):
                        j = (s - 17) // 2
                        act.wait_ge(s_tab, f - 2 + j + 1)
                        nc.scalar.activation(side["cos"][:, j, :], side["cos"][:, j, :], ACT.Sin).then_inc(s_sin, 1)
                    if 12 <= s < 16:
                        square_chunk(q_next, s - 12)
                for k in range(4, 8):
                    square_chunk(q_next, k)

            def out_phase(name, q_next):
                nb = N0[name]
                for j in range(4):
                    split_hi(nb + 2 * j + 2)
                    if j < 3:
                        split_hi(nb + 2 * j + 3)
                    residual_squares(q_next, (2 * j, 2 * j + 1))

            def project(m, groups, bufs):
                nb, at = N0[f"proj{m}"], AT0[f"proj{m}"]
                n, tile, staged = nb, 0, 0
                rotated = 0

                def relus(x0):
                    for x in (x0, x0 + 1):
                        y, n = 12 * (m - 1) + x, (x // 4 + 2) * P
                        act.wait_ge(s_idxmm, y + 1)
                        if x >= 2:
                            act.wait_ge(s_idx, y - 1)
                        nc.scalar.activation(work[:, x % 2, 0:n], bank[6 + x % 2][:, 0:n], ACT.Relu).then_inc(s_relu, 1)

                turning = []
                for g, (slabs, tiles) in enumerate(groups + [(0, [])]):
                    if m and g == 3:
                        act.wait_ge(s_iw, m)
                        nc.scalar.activation(bufs["wi"][:].rearrange("p b h -> p (b h)"), bank[6][:, 0:16], ACT.Copy)\
                            .then_inc(s_wi, 1)
                    for j in range(slabs):
                        if m and 4 <= g <= 6:
                            relus(4 * (g - 4) + 2 * j)
                        split_hi(n + 2 + j)
                    n += slabs
                    for kind, idx in turning:
                        act.wait_ge(s_rot, RO0[m] + rotated + 1)
                        if kind == "ik":
                            nc.scalar.activation(bufs["ikTh"][HD:P, 0, :], bufs["rot"][0:HD, rotated % 2, :], ACT.Copy)
                            nc.scalar.activation(bufs["ikTh"][0:HD, 0, :], bufs["rot"][0:HD, rotated % 2, :], ACT.Copy)\
                                .then_inc(s_roth, 1)
                        else:
                            nc.scalar.activation(bufs[kind + "Th"][:, idx, :], bufs["rot"][:, rotated % 2, :], ACT.Copy)\
                                .then_inc(s_roth, 1)
                        rotated += 1
                    turning = [t for t in tiles if t[0] in ROTATED]
                    for kind, idx in tiles:
                        act.wait_ge(s_used, n)
                        src = bank[2 * (g % 2) + idx % 2][:]
                        if kind == "u":
                            nc.scalar.activation(bufs["uT"][:, idx, :], src, ACT.Gelu).then_inc(s_actT, 1)
                            continue
                        if staged >= 2:
                            act.wait_ge(s_post, PO0[m] + staged - 1)
                        if kind in ROTATED:
                            if kind == "ik":
                                rows = slice(HD, HD + IDX_HEADS)
                                nc.scalar.activation(bufs["score"][rows, 0:S], src[rows, :], ACT.Copy).then_inc(s_iwT, 1)
                            nc.scalar.activation(bufs["st_hi"][:, staged % 2, :], src, ACT.Copy).then_inc(s_actT, 1)
                        else:
                            nc.scalar.activation(bufs["st_v"][:, staged % 2, :], src,
                                                 ACT.Gelu if kind == "va" else ACT.Copy).then_inc(s_actT, 1)
                        staged += 1

            def attention(m):
                t = ATT[m]
                u0, b_, nu, nh = t["u0"], t["b"], t["nu"], t["nh"]
                v_per_unit = nh // 8
                act.wait_ge(s_post, PO0[m] + (24 if m == 0 else 19))

                def probs_hi(u):
                    h, b = u // 4, u % 4
                    act.wait_ge(s_tr, u0 + u + 1)
                    if b == 0 and h >= 2:
                        act.wait_ge(s_pv, t["h0"] + h - 1)
                    dst = b_["PTh"][:, h % 2, :].rearrange("p (n q) -> p n q", q=P)[:, b:b + 3 * b + 1:3, :]
                    nc.scalar.activation(dst, bank[2 + u % 2][:, 0:(b + 1) * P].rearrange("p (n q) -> p n q", q=P), ACT.Copy)\
                        .then_inc(s_pth, 1)

                def o_out(h):
                    act.wait_ge(s_pv, t["h0"] + h + 1)
                    rows = slice(HD * (h % 2), HD * (h % 2) + HD)
                    nc.scalar.activation(b_["oT"][rows, h // 2, :], bank[4 + h % 2][0:HD, :], ACT.Copy).then_inc(s_o, 1)

                for u in range(nu):
                    b = u % 4
                    n = (b + 1) * P
                    if u < 4:
                        for c in range(v_per_unit * u, v_per_unit * (u + 1)):
                            nc.scalar.activation(h_hi[:, c + (4 if m else 0), :].rearrange("p (b d) -> p b d", d=P),
                                                 b_["vN"][:, :, c * P:(c + 1) * P], ACT.Copy).then_inc(s_vh, 1)
                    act.wait_ge(s_masked, u0 + u + 1)
                    if u >= 2:
                        act.wait_ge(s_tr, u0 + u - 1)
                    nc.scalar.activation(b_["P"][:, u % 2, 0:n], bank[SCORE_BANKS[u % 3]][:, 0:n], ACT.Exp, scale=-1.0,
                                         bias=b_["nmx"][:, u:u + 1], accum_out=b_["den"][:, u:u + 1]).then_inc(s_exp, 1)
                    if u:
                        probs_hi(u - 1)
                    if u % 4 == 2 and u >= 4:
                        o_out(u // 4 - 1)
                    if m and u % 4 == 2 and u // 4 < SGU_GROUPS:
                        g = u // 4
                        act.wait_ge(s_sgu, 4 * (m - 1) + g + 1)
                        nc.scalar.activation(h_hi[:, g, :], work[:, 2 + g % 2, :], ACT.Copy).then_inc(s_hhi, 1)
                probs_hi(nu - 1)
                if m == 0:
                    act.wait_ge(s_aw, 1)
                    nc.scalar.activation(a1["fine"][:, 1], a1["fine"][:, 0], ACT.Exp).then_inc(s_ae, 1)
                o_out(nh - 1)
                act.wait_ge(s_otr, OT0[m] + 1)
                nc.scalar.activation(b_["cTh"][0:nh, :], bank[6][0:nh, :], ACT.Copy).then_inc(s_ch, 1)
                for n in range(nh // 2):
                    act.wait_ge(s_on, OT0[m] + n + 2)
                    nc.scalar.activation(h_hi[:, n + (4 if m else 0), :], work[:, n % 2, :], ACT.Copy).then_inc(s_hhi, 1)

            act.dma_start(squares[:], squares_c.rearrange("p (n c) -> p n c", c=P)).then_inc(s_const, 16)
            act.dma_start(small[:], small_c).then_inc(s_const, 16)
            vectors = [("norm_mix", norm_mix), ("norm_ffn", norm_ffn), ("pool_scale", pool_scale), ("c", c_2),
                       ("f1", norm_ffn1_2), ("mix2", norm_mix_2), ("f2", norm_ffn2_2)]
            for name, v in vectors:
                n = v.shape[0] * KC
                r = VEC_ROWS[name]
                act.dma_start(vrows[r:r + n, :], v.rearrange("l (k p) -> (l k) p", p=P)).then_inc(s_vecs, 16)
            for name, v in (("norm_final", norm_final), ("final2", final_norm_2)):
                r = VEC_ROWS[name]
                act.dma_start(vrows[r:r + KC, :], v.rearrange("(k p) -> k p", p=P)).then_inc(s_vecs, 16)
            for l in range(2):
                act.dma_start(brows[0:N_MOD * KC, l, :],
                               ada_b_2[l].rearrange("(k p) -> k p", p=P)).then_inc(s_vecs, 16)

            split_hi(0)
            split_hi(1)
            residual_squares(0, range(8))
            act.wait_ge(s_setup, 1)
            link(nc.scalar.activation(vec[:], bank[4][:, 0:N_VEC], ACT.Copy))
            nc.scalar.activation(adab[:], bank[5][:, 0:2 * N_MOD * KC], ACT.Copy)
            nc.scalar.activation(cact[:], vec[:, VEC_ROWS["c"]:VEC_ROWS["c"] + KC], ACT.Silu).then_inc(s_vec, 1)
            norm_tail(0, "n0", None)

            nb = N0["pool_in"]

            def pool_hi(j):
                for n, c in enumerate((6 - 2 * j, 7 - 2 * j)):
                    act.wait_ge(s_win, 2 * j + n + 1)
                    nc.scalar.activation(p_hi[:, c, :], pP[:, n, :], ACT.Copy).then_inc(s_phi, 1)

            for j in range(4):
                split_hi(nb + 2 * j + 2)
                split_hi(nb + 2 * j + 3)
                for c in (6 - 2 * j, 7 - 2 * j):
                    act.wait_ge(s_used, nb + 2 * j + 2)
                    nc.scalar.activation(uP[:, c, :], bank[2 * (j % 2) + c % 2][:], ACT.Copy).then_inc(s_actT, 1)
                if j:
                    pool_hi(j - 1)
            pool_hi(3)
            nb = N0["group"]
            for j in range(2):
                split_hi(nb + j + 2)
                for c in range(4 - 4 * j, 8 - 4 * j):
                    act.wait_ge(s_used, nb + j + 1)
                    r = VEC_ROWS["pool_scale"] + c
                    nc.scalar.activation(act_hi[:, c ^ 4, :], bank[c][:], ACT.Identity, scale=vec[:, r:r + 1]).then_inc(s_ahi, 1)
            out_phase("pool_out", 1)
            norm_tail(1, "n1", None)
            ffn(0, 2)
            norm_tail(2, "n2", None)
            project(0, A1_GROUPS, a1)
            attention(0)
            out_phase("out0", 3)
            norm_tail(3, "n3", None)
            ffn(1, 4)
            norm_tail(4, None, None)
            residual_squares(5, range(8))
            norm_tail(5, "n5", 0)
            for l in range(2):
                q = 5 + 3 * l
                ffn(2 + 2 * l, q + 1)
                norm_tail(q + 1, ["n6", "n9"][l], 72 * l + 24)
                project(1 + l, A2_GROUPS, a2)
                attention(1 + l)
                out_phase(f"out{1 + l}", q + 2)
                norm_tail(q + 2, ["n7", "n10"][l], 72 * l + 48)
                ffn(3 + 2 * l, q + 3)
                if l == 0:
                    norm_tail(8, "n8", 72)
            norm_tail(11, None, None)

        @block.vector
        def _(dve):
            steps = [0]
            V = nc.vector

            def link(ins):
                steps[0] += 1
                ins.then_inc(s_dve, 1)
                dve.wait_ge(s_dve, steps[0])

            def split_lo(nb, i=0):
                if nb >= n_slabs:
                    return
                dve.wait_ge(s_hi, nb + 1 + 4 * i)
                V.tensor_tensor(w_lo[:, nb % SPL, :], raw[:, nb % RAW, :], w_hi[:, nb % SPL, :].bitcast(F32),
                                ALU.subtract).then_inc(s_lo, 1)

            def add_square(q, k):
                if k == 0:
                    return
                dve.wait_ge(s_sq, 8 * q + k + 1)
                if k > 1:
                    dve.wait_ge(s_sum, 7 * q + k - 1)
                V.tensor_tensor(sumsq[:], sumsq[:], sq[:, (7 * q + k - 1) % 2, :], ALU.add).then_inc(s_sum, 1)

            def norm_tail(q, hname, gains, shift=None):
                inv, hi, lo = sd4[:, 1, :], sd4[:, 2, :], sd4[:, 3, :]
                eye = ident.unsqueeze(1).to_broadcast([P, NB, P])
                dve.wait_ge(s_sd, q + 1)
                link(V.reciprocal(inv, sd4[:, 0, :]))
                link(V.tensor_copy(hi.bitcast(FR), inv))
                V.tensor_tensor(lo, inv, hi, ALU.subtract)
                V.tensor_tensor(diag_hi[:], eye, hi.unsqueeze(2).to_broadcast([P, NB, P]), ALU.mult).then_inc(s_rstd, 1)
                dve.wait_ge(s_rstd, 2 * q + 1)
                V.tensor_tensor(diag_lo[:], eye, lo.unsqueeze(2).to_broadcast([P, NB, P]), ALU.mult).then_inc(s_rstd, 1)
                if q in LATE:
                    split_lo(N0[LATE[q]] + 1)
                dve.wait_ge(s_spread, q + 1)
                rstd = bank[6]
                if hname is None:
                    dst = xT if q == 4 else yT
                    for k in range(KC):
                        V.scalar_tensor_tensor(out=dst[:, k, :], in0=xT[:, k, :], scalar=gains[:, k:k + 1], in1=rstd[:],
                                               op0=ALU.mult, op1=ALU.mult).then_inc(s_x, 1)
                    return
                base, ht = H0[hname], HT0[hname]
                for k in range(KC + 1):
                    if k < KC:
                        if k >= 4:
                            dve.wait_ge(s_hlo, base + k - 3)
                        V.scalar_tensor_tensor(out=work[:, k % 4, :], in0=xT[:, k, :], scalar=gains[:, k:k + 1],
                                               in1=rstd[:], op0=ALU.mult, op1=ALU.mult).then_inc(s_htmp, 1)
                    if k:
                        c = k - 1
                        dve.wait_ge(s_hhi, base + c + 1)
                        sh = 0.0 if shift is None else mod[:, shift + c:shift + c + 1]
                        V.scalar_tensor_tensor(out=h_lo[:, c, :], in0=work[:, c % 4, :], scalar=sh,
                                               in1=h_hi[:, c, :].bitcast(F32), op0=ALU.add, op1=ALU.subtract)\
                            .then_inc(s_hlo, 1)

            def residual(c, src, gate):
                V.scalar_tensor_tensor(out=xT[:, c, :], in0=src, scalar=1.0 if gate is None else gate[:, c:c + 1],
                                       in1=xT[:, c, :], op0=ALU.mult, op1=ALU.add).then_inc(s_x, 1)

            def ffn(f, q_next, gate):
                nb, at, dt, aa = N0[f"ffn{f}"], AT0[f"ffn{f}"], DT0[f"ffn{f}"], ACT0[f]

                def ada_half(i, half):
                    dve.wait_ge(s_adaload[half], 16 * (N_MOD * f + 1) + 16 * i)
                    for j in range(4):
                        k = 4 * half + j
                        if k:
                            dve.wait_ge(s_adastep, 8 * N_MOD * f + k + 8 * i)
                        w = ada_w[:, half, j, :]
                        if k == 0:
                            ins = V.tensor_scalar(ada_acc[:], w, cact[:, 0:1], None, ALU.mult)
                        else:
                            ins = V.scalar_tensor_tensor(out=ada_acc[:], in0=w, scalar=cact[:, k:k + 1], in1=ada_acc[:],
                                                         op0=ALU.mult, op1=ALU.add)
                        ins.then_inc(s_adastep, 1)

                def body(i, ada):
                    split_lo(nb + 2, i)
                    if ada:
                        ada_half(i, 0)
                    split_lo(nb + 3, i)
                    if ada:
                        ada_half(i, 1)
                    split_lo(nb + 4, i)
                    split_lo(nb + 5, i)
                    dve.wait_ge(s_alo, aa + 2 * i)
                    for c in range(2):
                        dve.wait_ge(s_used, nb + 4 + 4 * i)
                        dve.wait_ge(s_actT, at + c + 1 + 2 * i)
                        V.tensor_tensor(work[:, 2 + c, :], work[:, c, :], bank[2 + c][:], ALU.mult).then_inc(s_dveT, 1)
                    for c in range(2):
                        dve.wait_ge(s_ahi, aa + c + 1 + 2 * i)
                        V.tensor_tensor(act_lo[:, bass.ds(i * 2 + c, 1), :], work[:, 2 + c:3 + c, :],
                                        act_hi[:, bass.ds(i * 2 + c, 1), :].bitcast(F32), ALU.subtract).then_inc(s_alo, 1)
                    if ada:
                        dve.wait_ge(s_adamm, N_MOD * f + 1 + i)
                        V.tensor_tensor(mod[:, bass.ds(i * 4 + 4 * N_MOD * f, 4)], bank[6][:, 0:4],
                                        adab[:, bass.ds(i * 4 + 4 * N_MOD * f, 4)], ALU.add).then_inc(s_mod, 1)

                if f < 4:
                    with dve.Fori(0, N_MOD) as i:
                        body(i, True)
                    with dve.Fori(N_MOD, NF // 2) as i:
                        body(i, False)
                else:
                    with dve.Fori(0, NF // 2) as i:
                        body(i, False)
                if f == 1:
                    modulation_gains(0)
                if f == 3:
                    modulation_gains(1)

                def down_done(half, c):
                    if c < 3:
                        dve.wait_ge(s_down, 6 * f + 3 * half + c + 1)
                    else:
                        dve.wait_ge(s_used, nb + 44 + 11 * (half + 1))

                for s in range(22):
                    if s < 21:
                        split_lo(nb + 44 + s + 2)
                    if f in (2, 4) and 15 <= s < 20:
                        rope_tables(f // 2, s - 15)
                    if 11 <= s < 15:
                        c = s - 11
                        down_done(0, c)
                        residual(c, bank[4 + c][:], gate)
                    if 12 <= s < 16:
                        add_square(q_next, s - 12)
                for c in range(4, 8):
                    down_done(1, c - 4)
                    residual(c, bank[c - 4][:], gate)
                    if c > 4:
                        add_square(q_next, c - 1)
                add_square(q_next, 7)

            def modulation_gains(l):
                m = 72 * l
                dve.wait_ge(s_mod, 18 * (l + 1))
                for n, (vecname, sc) in enumerate((("f1", 8), ("mix2", 32), ("f2", 56))):
                    r = VEC_ROWS[vecname] + 8 * l
                    V.scalar_tensor_tensor(out=coefs[:, l, n, :], in0=mod[:, m + sc:m + sc + 8], scalar=1.0,
                                           in1=vec[:, r:r + 8], op0=ALU.add, op1=ALU.mult)
                V.tensor_scalar(coefs[:, l, 3, :], mod[:, m + 16:m + 24], 0.5, None, ALU.mult)
                link(V.tensor_scalar(coefs[:, l, 4, :], mod[:, m + 64:m + 72], 0.5, None, ALU.mult))

            def out_phase(name, q_next, gate):
                nb, dt = N0[name], DT0[name]
                for j in range(4):
                    split_lo(nb + 2 * j + 2)
                    if j < 3:
                        split_lo(nb + 2 * j + 3)
                    for c in (2 * j, 2 * j + 1):
                        dve.wait_ge(s_used, nb + 2 * j + 2)
                        residual(c, bank[OUT_BANK[name] + c % 4][:], gate)
                        if c:
                            add_square(q_next, c - 1)
                add_square(q_next, 7)

            def rope_tables(m, step):
                pi = float(np.float32(3.1415925))
                r, ang, t, pos = (side["ang"][:, j, :] for j in range(4))
                if step == 0:
                    dve.wait_ge(s_pos, 16 * m)
                    link(V.tensor_copy(t, pos.bitcast(I32)))
                    link(V.tensor_scalar(ang, t, small[:, 64:65], None, ALU.mult))
                    return
                j, quarter = (0, 0.25) if step <= 2 else (1, 0.0)
                if step % 2:
                    magic = 1.5 * 2.0 ** 23
                    link(V.tensor_scalar(t, ang, 1.0 / (2.0 * np.pi), quarter, ALU.mult, ALU.add))
                    link(V.tensor_scalar(t, t, magic, None, ALU.add))
                    link(V.tensor_scalar(t, t, -magic, None, ALU.add))
                    return
                src = ang
                for part in two_pi_parts():
                    link(V.scalar_tensor_tensor(out=r, in0=t, scalar=-part, in1=src, op0=ALU.mult, op1=ALU.add))
                    src = r
                if quarter:
                    link(V.tensor_scalar(r, r, float(np.pi / 2), None, ALU.add))
                V.tensor_scalar(side["cos"][:, j, :], r, pi, -pi, ALU.min, ALU.max).then_inc(s_tab, 1)
                dve.wait_ge(s_tab, 2 * (m - 1) + j + 1)

            def project(m, groups, bufs):
                nb = N0[f"proj{m}"]
                n, post = nb, [0]
                pending = []
                dve.wait_ge(s_phaseld, PHASE_LD[m])

                def posts(tiles):
                    for kind, idx in tiles:
                        j = post[0]
                        post[0] += 1
                        aux = bank[4 + j % 2]
                        if kind in ("v", "va"):
                            dve.wait_ge(s_postmm, PO0[m] + j + 1)
                            dst = bufs["vN" if kind == "v" else "vaN"][:, :, idx * P:(idx + 1) * P]
                            V.tensor_copy(dst, aux[:].rearrange("p (b d) -> p b d", d=P)).then_inc(s_post, 1)
                            continue
                        i = rotated[0]
                        rotated[0] += 1
                        rot = bufs["rot"][:, i % 2, :]
                        dve.wait_ge(s_postmm, PO0[m] + j + 1)
                        if i:
                            dve.wait_ge(s_rot, RO0[m] + i)
                        link(V.tensor_tensor(bufs["turned"][:], aux[:], bufs["cos"][:, 1, :], ALU.mult))
                        V.tensor_tensor(rot, rot, bufs["turned"][:], ALU.add).then_inc(s_rot, 1)
                        dve.wait_ge(s_roth, RO0[m] + i + 1)
                        if kind == "ik":
                            V.tensor_tensor(bufs["ikTl"][HD:P, 0, :], rot[0:HD, :], bufs["ikTh"][0:HD, 0, :].bitcast(F32), ALU.subtract)
                            V.tensor_tensor(bufs["ikTl"][0:HD, 0, :], rot[0:HD, :], bufs["ikTh"][0:HD, 0, :].bitcast(F32),
                                            ALU.subtract).then_inc(s_post, 1)
                        else:
                            V.tensor_tensor(bufs[kind + "Tl"][:, idx, :], rot, bufs[kind + "Th"][:, idx, :].bitcast(F32),
                                            ALU.subtract).then_inc(s_post, 1)

                def take_rotated(g, tiles, first):
                    for c, (kind, idx) in enumerate(tiles):
                        if kind not in ROTATED:
                            continue
                        j, i = staged[0], taken[0]
                        staged[0] += 1
                        taken[0] += 1
                        src = bank[2 * (g % 2) + idx % 2][:]
                        dve.wait_ge(s_actT, AT0[f"proj{m}"] + first + c + 1)
                        V.tensor_tensor(bufs["st_lo"][:, j % 2, :], src, bufs["st_hi"][:, j % 2, :].bitcast(F32), ALU.subtract)
                        if m:
                            dve.wait_ge(s_sin, 2 * m)
                        if i >= 2:
                            dve.wait_ge(s_post, PO0[m] + i - 1)
                        V.tensor_tensor(bufs["rot"][:, i % 2, :], src, bufs["cos"][:, 0, :], ALU.mult).then_inc(s_dveT2, 1)

                staged, taken, rotated, first = [0], [0], [0], 0
                two = [((2, 3), 2)]
                ROUNDS = {5: ([((1,), 1)], [((1,), 1)]), 6: ([((1,), 2)], [((1,), 3)]),
                          7: ([((1,), 4)], [((1, 2, 3), 1), ((1,), 4)]),
                          8: (two, two), 9: (two, two), 10: (two, two), 11: (two, [((2, 3), 1)])}

                def index_sums(x0):
                    for x in (x0, x0 + 1):
                        y, b, h = 12 * (m - 1) + x, x // 4 + 1, x % 4
                        w = bufs["score"][:, TRI[b]:TRI[b + 1]]
                        dve.wait_ge(s_relu, y + 1)
                        if x == 0:
                            dve.wait_ge(s_phaseld, PHASE_LD[m])
                            dve.wait_ge(s_wi, m)
                        if y:
                            dve.wait_ge(s_idx, y)
                        V.scalar_tensor_tensor(out=w, in0=work[:, x % 2, 0:(b + 1) * P], scalar=bufs["wi"][:, b, h:h + 1],
                                               in1=bufs["causal"][:, TRI[b]:TRI[b + 1]] if h == 0 else w,
                                               op0=ALU.mult, op1=ALU.add).then_inc(s_idx, 1)
                for g, (slabs, tiles) in enumerate(groups):
                    for j in range(slabs):
                        if m and 4 <= g <= 6:
                            index_sums(4 * (g - 4) + 2 * j)
                        split_lo(n + 2 + j)
                        if m and g >= 5:
                            if g <= 7 and j == 0:
                                dve.wait_ge(s_idx, 12 * (m - 1) + 4 * (g - 4))
                            for blocks, rounds in ROUNDS[g][j]:
                                for _ in range(rounds):
                                    topk_round(bufs, blocks)
                    n += slabs
                    posts([t for t in pending if t[0] != "u"])
                    take_rotated(g, tiles, first)
                    first += len(tiles)
                    pending = tiles
                    if m and g == 2:
                        dve.wait_ge(s_wtr, m)
                        V.tensor_tensor(bufs["wT"][:], bank[7][:].rearrange("p (g t) -> p g t", t=P),
                                        upper.unsqueeze(1).to_broadcast([P, 4, P]), ALU.mult).then_inc(s_wT, 1)
                posts([t for t in pending if t[0] != "u"])
                if m:
                    for b in range(1, NB):
                        V.tensor_scalar(bufs["masks"][:, 0, TRI[b]:TRI[b + 1]], bufs["score"][:, TRI[b]:TRI[b + 1]],
                                        -2e38, NEG, ALU.is_gt, ALU.mult).then_inc(s_mask, 1)
                    dve.wait_ge(s_mask, 3 * m)

            def topk_round(bufs, blocks):
                for b in blocks:
                    ins = V.max(bufs["m8"][:, b - 1, :], bufs["score"][:, TRI[b]:TRI[b + 1]])
                    steps[0] += 1
                    ins.then_inc(s_dve, 1)
                for n, b in enumerate(blocks):
                    dve.wait_ge(s_dve, steps[0] - len(blocks) + 1 + n)
                    w = bufs["score"][:, TRI[b]:TRI[b + 1]]
                    ins = V.match_replace(out=w, in_to_replace=bufs["m8"][:, b - 1, :], in_values=w, imm_value=TAKEN)
                    ins.then_inc(s_dve, 1)
                steps[0] += len(blocks)
                dve.wait_ge(s_dve, steps[0])

            def sgu(m, bufs, g):
                dve.wait_ge(s_sgumm, 4 * (m - 1) + g + 1)
                dve.wait_ge(s_actT, AT0[f"proj{m}"] + 20 + g)
                dst = work[:, 2 + g % 2, :]
                if g >= 2:
                    dve.wait_ge(s_hlo, H0[f"attn{m}"] + g - 1)
                link(V.tensor_tensor(dst.rearrange("p (n t) -> p n t", t=P), bank[7][:].rearrange("p (n t) -> p n t", t=P),
                                     bufs["bbc"][:, g:g + 1, :].to_broadcast([P, NB, P]), ALU.add))
                V.tensor_tensor(dst, dst, bufs["uT"][:, g, :], ALU.mult).then_inc(s_sgu, 1)

            def sgu_lo(m, g):
                dve.wait_ge(s_hhi, H0[f"attn{m}"] + g + 1)
                V.tensor_tensor(h_lo[:, g, :], work[:, 2 + g % 2, :], h_hi[:, g, :].bitcast(F32), ALU.subtract).then_inc(s_hlo, 1)

            def attention(m):
                t = ATT[m]
                u0, bufs, nu, nh = t["u0"], t["b"], t["nu"], t["nh"]

                def mask_scores(u):
                    h, b = u // 4, u % 4
                    n = (b + 1) * P
                    g = [i for i, (lo, hi) in enumerate(HEAD_GROUPS) if lo <= h < hi][0] if m == 0 else 0
                    dve.wait_ge(s_scmm, u0 + u + 1)
                    scores = bank[SCORE_BANKS[u % 3]][:, 0:n]
                    V.tensor_tensor_reduce(out=scores, in0=scores,
                                           in1=bufs["masks"][:, g, TRI[b]:TRI[b + 1]], scale=-(HD ** -0.5), scalar=3e38,
                                           op0=ALU.add, op1=ALU.min, accum_out=bufs["nmx"][:, u:u + 1]).then_inc(s_masked, 1)

                def probs_lo(u):
                    h, b = u // 4, u % 4
                    dve.wait_ge(s_pth, u0 + u + 1)
                    hi = bufs["PTh"][:, h % 2, :].rearrange("p (n q) -> p n q", q=P)[:, b:b + 3 * b + 1:3, :]
                    lo = bufs[f"PTl{h % 2}"][:].rearrange("p (n q) -> p n q", q=P)[:, b:b + 3 * b + 1:3, :]
                    V.tensor_tensor(lo, bank[2 + u % 2][:, 0:(b + 1) * P].rearrange("p (n q) -> p n q", q=P),
                                    hi.bitcast(F32), ALU.subtract).then_inc(s_pt, 1)

                v_per_unit = nh // 8
                for u in range(3):
                    mask_scores(u)
                for u in range(nu):
                    if u < 4:
                        for c in range(v_per_unit * u, v_per_unit * (u + 1)):
                            dve.wait_ge(s_vh, V0[m] + c + 1)
                            cc = c + (4 if m else 0)
                            V.tensor_tensor(h_lo[:, cc, :].rearrange("p (b d) -> p b d", d=P), bufs["vN"][:, :, c * P:(c + 1) * P],
                                            h_hi[:, cc, :].bitcast(F32).rearrange("p (b d) -> p b d", d=P), ALU.subtract)\
                                .then_inc(s_vl, 1)
                    if u == 4:
                        dve.wait_ge(s_vl, V0[m] + nh // 2)
                    if u + 3 < nu:
                        mask_scores(u + 3)
                    probs_lo(u)
                    if u == nu - 8:
                        dve.wait_ge(s_hlo, H0[f"attn{m}"] + (4 if m else 0))
                        V.tensor_copy(sel[0:nh, 0:nh, :], ident[0:nh, 0:nh].unsqueeze(2).to_broadcast([nh, nh, HD])).then_inc(s_sel, 1)
                    if m and u // 4 < SGU_GROUPS:
                        if u % 4 == 0:
                            sgu(m, bufs, u // 4)
                        if u % 4 == 2:
                            sgu_lo(m, u // 4)
                den = bufs["den"][:, 0:nu].rearrange("p (h b) -> p b h", b=NB)
                nmx = bufs["nmx"][:, 0:nu].rearrange("p (h b) -> p b h", b=NB)
                dve.wait_ge(s_exp, u0 + nu)
                F = bufs["fine"]
                if m == 0:
                    least, ex, wsum, tot = F[:, 2, :, 0:1], F[:, 1], F[:, 3, :, 0:3], F[:, 4, :, 0:1]
                    link(V.tensor_reduce(least, nmx, AX_X, ALU.min))
                    V.tensor_tensor(F[:, 0], least.to_broadcast([P, NB, 16]), nmx, ALU.subtract).then_inc(s_aw, 1)
                    dve.wait_ge(s_ae, 1)
                    link(V.tensor_tensor(ex, ex, den, ALU.mult))
                    for g, (lo, hi) in enumerate(HEAD_GROUPS):
                        link(V.tensor_reduce(F[:, 3, :, g:g + 1], ex[:, :, lo:hi], AX_X, ALU.add))
                        link(V.tensor_scalar(F[:, 3, :, g:g + 1], F[:, 3, :, g:g + 1], 1.0 / (hi - lo), None, ALU.mult))
                    link(V.tensor_reduce(tot, wsum, AX_X, ALU.add))
                    link(V.reciprocal(tot, tot))
                    link(V.tensor_scalar(tot, tot, float(len(HEAD_GROUPS)), None, ALU.mult))
                    link(V.tensor_tensor(wsum, wsum, tot.to_broadcast([P, NB, 3]), ALU.mult))
                    link(V.reciprocal(F[:, 5], den))
                    for g, (lo, hi) in enumerate(HEAD_GROUPS):
                        last = V.tensor_tensor(F[:, 5, :, lo:hi], F[:, 5, :, lo:hi],
                                               F[:, 3, :, g:g + 1].to_broadcast([P, NB, hi - lo]), ALU.mult)
                    last.then_inc(s_on, 1)
                else:
                    V.reciprocal(F[:, 5, :, 0:nh], den).then_inc(s_on, 1)
                dve.wait_ge(s_ch, m + 1)
                V.tensor_tensor(bufs["cTl"][0:nh, :], bank[6][0:nh, :], bufs["cTh"][0:nh, :].bitcast(F32), ALU.subtract).then_inc(s_cl, 1)
                dve.wait_ge(s_o, t["h0"] + nh)
                c0, base = 4 if m else 0, H0[f"attn{m}"]
                for n in range(nh // 2 + 1):
                    if n < nh // 2:
                        dve.wait_ge(s_otr, OT0[m] + n + 2)
                        if n >= 2:
                            dve.wait_ge(s_hlo, base + c0 + n - 1)
                        V.tensor_tensor(work[:, n % 2, :], bufs["oT"][:, n, :], bank[7 - n % 2][:], ALU.mult).then_inc(s_on, 1)
                    if n:
                        c = c0 + n - 1
                        dve.wait_ge(s_hhi, base + c + 1)
                        V.tensor_tensor(h_lo[:, c, :], work[:, (n - 1) % 2, :], h_hi[:, c, :].bitcast(F32), ALU.subtract)\
                            .then_inc(s_hlo, 1)

            V.memset(ones[:], 1.0 / D).then_inc(s_ones, 1)
            V.memset(ones_r[:].bitcast(F32), 1.0).then_inc(s_ones, 1)
            for k in range(KC):
                dve.wait_ge(s_xtr, k + 1)
                V.tensor_copy(xT[:, k, :], bank[k % 4][:]).then_inc(s_x, 1)
                add_square(0, k - 1) if k else None
            add_square(0, 7)
            dve.wait_ge(s_const, 32)
            V.tensor_copy(turn_hi[:], squares[:, 1:3, :]).then_inc(s_ones, 1)
            split_lo(0)
            split_lo(1)
            dve.wait_ge(s_vec, 1)

            def gain(name, l=0):
                r = VEC_ROWS[name] + 8 * l
                return vec[:, r:r + 8]

            norm_tail(0, "n0", gain("norm_mix", 0))
            nb = N0["pool_in"]

            def window(j):
                g = 3 - j
                for n, c in enumerate((6 - 2 * j, 7 - 2 * j)):
                    t = 2 * j + n
                    dve.wait_ge(s_actT, t + 1)
                    if t:
                        dve.wait_ge(s_win, t)
                    src = uP[:, c, :]
                    for step in range(g + 1):
                        sh, dst = 2 ** step, winA[:, step % 2, :]
                        V.tensor_copy(dst[:, 0:sh], src[:, 0:sh])
                        link(V.tensor_tensor(dst[:, sh:S], src[:, sh:S], src[:, 0:S - sh], ALU.add))
                        src = dst
                    link(V.tensor_tensor(src[:, 0:16], src[:, 0:16], small[:, 16 * g:16 * g + 16], ALU.mult))
                    if j:
                        dve.wait_ge(s_plo, t - 1)
                    V.scalar_tensor_tensor(out=pP[:, n, :], in0=src, scalar=1.0 / POOL_WINDOWS[g], in1=uP[:, c, :],
                                           op0=ALU.mult, op1=ALU.subtract).then_inc(s_win, 1)
                for n, c in enumerate((6 - 2 * j, 7 - 2 * j)):
                    dve.wait_ge(s_phi, 2 * j + n + 1)
                    V.tensor_tensor(p_lo[:, c, :], pP[:, n, :], p_hi[:, c, :].bitcast(F32), ALU.subtract).then_inc(s_plo, 1)

            for j in range(4):
                split_lo(nb + 2 * j + 2)
                split_lo(nb + 2 * j + 3)
                if j:
                    window(j - 1)
            window(3)
            nb = N0["group"]
            for j in range(2):
                split_lo(nb + j + 2)
                for n, c in enumerate(range(4 - 4 * j, 8 - 4 * j)):
                    dve.wait_ge(s_ahi, 4 * j + n + 1)
                    r = VEC_ROWS["pool_scale"] + c
                    V.scalar_tensor_tensor(out=act_lo[:, c ^ 4, :], in0=bank[c][:], scalar=vec[:, r:r + 1],
                                           in1=act_hi[:, c ^ 4, :].bitcast(F32), op0=ALU.mult, op1=ALU.subtract).then_inc(s_alo, 1)
            out_phase("pool_out", 1, None)
            norm_tail(1, "n1", gain("norm_ffn", 0))
            ffn(0, 2, None)
            norm_tail(2, "n2", gain("norm_mix", 1))
            project(0, A1_GROUPS, a1)
            attention(0)
            out_phase("out0", 3, None)
            norm_tail(3, "n3", gain("norm_ffn", 1))
            ffn(1, 4, None)
            norm_tail(4, None, gain("norm_final"))
            for k in range(1, KC):
                add_square(5, k)
            norm_tail(5, "n5", coefs[:, 0, 0, :], 0)
            for l in range(2):
                q = 5 + 3 * l
                ffn(2 + 2 * l, q + 1, coefs[:, l, 3, :])
                norm_tail(q + 1, ["n6", "n9"][l], coefs[:, l, 1, :], 72 * l + 24)
                project(1 + l, A2_GROUPS, a2)
                attention(1 + l)
                out_phase(f"out{1 + l}", q + 2, mod[:, 72 * l + 40:72 * l + 48])
                norm_tail(q + 2, ["n7", "n10"][l], coefs[:, l, 2, :], 72 * l + 48)
                ffn(3 + 2 * l, q + 3, coefs[:, l, 4, :])
                if l == 0:
                    norm_tail(8, "n8", coefs[:, 1, 0, :], 72)
            norm_tail(11, None, gain("final2"))
            for b in range(NB):
                for half in range(2):
                    n = 2 * b + half
                    dve.wait_ge(s_ytr, n + 1)
                    V.tensor_copy(y_nat[:, b, 512 * half:512 * half + 512], bank[n % 4][:]).then_inc(s_ynat, 1)

        @block.tensor
        def _(pe):
            T = nc.tensor

            def mm3(dst, wh, wl, mh, ml, first, last):
                T.matmul(dst, wh, mh, start=first, stop=False)
                T.matmul(dst, wh, ml, start=False, stop=False)
                return T.matmul(dst, wl, mh, start=False, stop=last)

            def slab(nb, c):
                return (w_hi[:, nb % SPL, :].rearrange("p (k c) -> p k c", c=c),
                        w_lo[:, nb % SPL, :].rearrange("p (k c) -> p k c", c=c))

            def pair(nb, banks, mh, ml, ready=None, i=0):
                for half in range(2):
                    half_pair(nb, half, banks, mh, ml, ready, i)

            def half_pair(nb, half, banks, mh, ml, ready=None, i=0):
                hi, lo = slab(nb + half, 256)
                pe.wait_ge(s_lo, nb + half + 1 + 4 * i)
                order = [(c, j) for c in range(2) for j in range(4)]
                if ready is not None:
                    order = [(c, j) for j in range(4) for c in range(2)]
                for c, j in order:
                    k = 4 * half + j
                    if ready is not None and c == 0:
                        pe.wait_ge(ready[0], ready[1] + k + 1)
                    ins = mm3(bank[banks[c]][:], hi[:, j, c * P:(c + 1) * P], lo[:, j, c * P:(c + 1) * P],
                              mh[:, k, :], ml[:, k, :], k == 0, k == KC - 1)
                ins.then_inc(s_used, 1)

            def keep_warm(n):
                for _ in range(n):
                    T.matmul(bank[4][:, 0:2 * P], ones_r[:], turn_hi[:].rearrange("p n c -> p (n c)"), start=True, stop=True)

            def mean(q):
                if q == 0:
                    pe.wait_ge(s_ones, 3)
                else:
                    pe.wait_ge(s_x, 8 * q + (5 if q == 1 else 4))
                    keep_warm(9)
                pe.wait_ge(s_sum, 7 * q + 7)
                for b in range(NB):
                    ins = T.matmul(bank[7][:, b:b + 1], sumsq[:, b * P:(b + 1) * P], ones[:, 0:1], start=True, stop=True)
                ins.then_inc(s_mean, 1)
                if q:
                    keep_warm(6)
                for n, d in enumerate((diag_hi, diag_lo)):
                    pe.wait_ge(s_rstd, 2 * q + n + 1)
                    ins = T.matmul(bank[6][:], ones_r[:], d[:].rearrange("p b t -> p (b t)"), start=n == 0, stop=n == 1)
                ins.then_inc(s_spread, 1)
                if q and q < 11:
                    keep_warm(48 if q == 4 else 10)

            def ffn(f, hname):
                nb, at, dt, aa = N0[f"ffn{f}"], AT0[f"ffn{f}"], DT0[f"ffn{f}"], ACT0[f]

                def body(i, ada, first=False):
                    if not first:
                        pe.wait_ge(s_actT, at + 2 * i)
                    pair(nb, (0, 1), h_hi, h_lo, (s_hlo, H0[hname]) if first else None, i)
                    if not first:
                        pe.wait_ge(s_dveT, dt + 2 * i)
                    pair(nb + 2, (2, 3), h_hi, h_lo, None, i)
                    if ada:
                        pe.wait_ge(s_adastep, 8 * N_MOD * f + 8 + 8 * i)
                        if not (f == 0 and first):
                            pe.wait_ge(s_mod, N_MOD * f + i)
                        for j in range(4):
                            ins = T.matmul(bank[6][:, j:j + 1], ada_acc[:, j * P:(j + 1) * P], small[:, 66:67],
                                           start=True, stop=True)
                        ins.then_inc(s_adamm, 1)

                body(0, f < 4, True)
                if f < 4:
                    with pe.Fori(1, N_MOD) as i:
                        body(i, True)
                    with pe.Fori(N_MOD, NF // 2) as i:
                        body(i, False)
                else:
                    with pe.Fori(1, NF // 2) as i:
                        body(i, False)

                def down(half, kk, i=0, loop=False, signal=False):
                    n = nb + 44 + 11 * half + kk
                    hi, lo = slab(n, 512)
                    pe.wait_ge(s_lo, n + 1 + 2 * i)
                    if half == 0:
                        pe.wait_ge(s_alo, aa + 2 * kk + 2 + 4 * i)
                    for c in range(4):
                        for j in range(2):
                            k = 2 * kk + j
                            if loop:
                                mh, ml = act_hi[:, bass.ds(i * 4 + k, 1), :], act_lo[:, bass.ds(i * 4 + k, 1), :]
                            else:
                                mh, ml = act_hi[:, k:k + 1, :], act_lo[:, k:k + 1, :]
                            dst = bank[(4 if half == 0 else 0) + c][:].rearrange("p (o s) -> p o s", o=1)
                            ins = mm3(dst, hi[:, j, c * P:(c + 1) * P],
                                      lo[:, j, c * P:(c + 1) * P], mh, ml, kk == 0 and j == 0, signal and j == 1)
                        if signal and c < 3:
                            ins.then_inc(s_down, 1)
                    ins.then_inc(s_used, 1)

                for half in range(2):
                    down(half, 0)
                    with pe.Fori(0, 4) as i:
                        down(half, 1, i, True)
                        down(half, 2, i, True)
                    down(half, 9)
                    down(half, 10, signal=True)

            def out_phase(name, mh, ml, ready, free):
                nb, dt = N0[name], DT0[name]
                for s, v in free:
                    pe.wait_ge(s, v)
                for j in range(4):
                    if j >= 2:
                        pe.wait_ge(s_x, free_x[name] + 2 * (j - 1))
                    first = OUT_BANK[name] + 2 * (j % 2)
                    pair(nb + 2 * j, (first, first + 1), mh, ml, ready if j == 0 else None)

            free_x = {"pool_out": 8, "out0": 24, "out1": 56, "out2": 80}

            def project(m, groups, bufs, hname):
                nb, at = N0[f"proj{m}"], AT0[f"proj{m}"]
                n, post, tiles_done = nb, [0], 0
                turn = turn_hi[:, min(m, 1), :]
                rotated = [0]
                pending = []
                counts, turned = [], []

                def posts(tiles):
                    for kind, idx, tile in tiles:
                        if kind == "u":
                            continue
                        j = post[0]
                        post[0] += 1
                        aux = bank[4 + j % 2]
                        pe.wait_ge(s_actT, at + tile + 1)
                        if j >= 2:
                            pe.wait_ge(s_post, PO0[m] + j - 1)
                        if kind in ("v", "va"):
                            for b in range(NB):
                                ins = T.transpose(aux[:, b * P:(b + 1) * P], bufs["st_v"][:, j % 2, b * P:(b + 1) * P], ident)
                        else:
                            T.matmul(aux[:], turn, bufs["st_hi"][:, j % 2, :], start=True, stop=False)
                            pe.wait_ge(s_dveT2, RO0[m] + rotated[0] + 1)
                            ins = T.matmul(aux[:], turn, bufs["st_lo"][:, j % 2, :], start=False, stop=True)
                            rotated[0] += 1
                        ins.then_inc(s_postmm, 1)

                def index_scores(x0):
                    for x in (x0, x0 + 1):
                        y, b, h = 12 * (m - 1) + x, x // 4 + 1, x % 4
                        if x >= 2:
                            pe.wait_ge(s_relu, y - 1)
                        r = slice(HD * (h % 2), HD * (h % 2) + HD)
                        q, k = slice(b * P, (b + 1) * P), slice(0, (b + 1) * P)
                        mm3(bank[6 + x % 2][:, k], bufs["iqTh"][r, h // 2, q], bufs["iqTl"][r, h // 2, q],
                            bufs["ikTh"][r, 0, k], bufs["ikTl"][r, 0, k], True, True).then_inc(s_idxmm, 1)

                for g, (slabs, tiles) in enumerate(groups):
                    between = None
                    if m and 4 <= g <= 6:
                        if g == 4:
                            pe.wait_ge(s_post, PO0[m] + 3)
                            pe.wait_ge(s_wi, m)
                            pe.wait_ge(s_wT, m)
                        index_scores(4 * (g - 4))
                        between = 4 * (g - 4) + 2
                    if g >= 2:
                        pe.wait_ge(s_actT, at + counts[g - 2])
                        pe.wait_ge(s_dveT2, RO0[m] + turned[g - 2])
                    if slabs == 2:
                        for half in range(2):
                            half_pair(n, half, (2 * (g % 2), 2 * (g % 2) + 1), h_hi, h_lo, (s_hlo, H0[hname]) if g == 0 else None)
                            if between is not None and half == 0:
                                index_scores(between)
                    else:
                        hi, lo = slab(n, P)
                        pe.wait_ge(s_lo, n + 1)
                        for k in range(KC):
                            ins = mm3(bank[2 * (g % 2)][:], hi[:, k, :], lo[:, k, :], h_hi[:, k, :], h_lo[:, k, :],
                                      k == 0, k == KC - 1)
                        ins.then_inc(s_used, 1)
                    n += slabs
                    posts(pending)
                    if m and g == 1:
                        pe.wait_ge(s_phaseld, PHASE_LD[m])
                        for w in range(4):
                            ins = T.transpose(bank[7][:, w * P:(w + 1) * P], bufs["sguw"][:, w, :], ident)
                        ins.then_inc(s_wtr, 1)
                    if m and g == 2:
                        pe.wait_ge(s_iwT, m)
                        rows = slice(HD, HD + IDX_HEADS)
                        for b in range(NB):
                            ins = T.transpose(bank[6][:, 4 * b:4 * b + 4], bufs["score"][rows, b * P:(b + 1) * P], ident[rows, rows])
                        ins.then_inc(s_iw, 1)
                    pending = [(k, i, tiles_done + j) for j, (k, i) in enumerate(tiles)]
                    tiles_done += len(tiles)
                    counts.append(tiles_done)
                    turned.append((turned[-1] if turned else 0) + sum(k in ROTATED for k, _ in tiles))
                posts(pending)

            def sgu(m, bufs, g):
                if g:
                    pe.wait_ge(s_sgu, 4 * (m - 1) + g)
                for b in range(NB):
                    ins = T.matmul(bank[7][:, b * P:(b + 1) * P], bufs["vaN"][:, b, g * P:(g + 1) * P],
                                   bufs["wT"][:, g, :], start=True, stop=True)
                ins.then_inc(s_sgumm, 1)

            def attention(m):
                t = ATT[m]
                u0, bufs, nu, nh = t["u0"], t["b"], t["nu"], t["nh"]
                n_post = 24 if m == 0 else 19
                pe.wait_ge(s_post, PO0[m] + n_post)
                pe.wait_ge(s_actT, AT0[f"out{m}"])

                def scores(u):
                    h, b = u // 4, u % 4
                    if u >= 3:
                        pe.wait_ge(s_exp, u0 + u - 2)
                    r = slice(HD * (h % 2), HD * (h % 2) + HD)
                    q, k = slice(b * P, (b + 1) * P), slice(0, (b + 1) * P)
                    mm3(bank[SCORE_BANKS[u % 3]][:, k], bufs["qTh"][r, h // 2, q], bufs["qTl"][r, h // 2, q],
                        bufs["kTh"][r, h // 2, k], bufs["kTl"][r, h // 2, k], True, True).then_inc(s_scmm, 1)

                def values(h):
                    c = h // 2
                    pe.wait_ge(s_pt, u0 + 4 * h + 4)
                    pe.wait_ge(s_vl, V0[m] + c + 1)
                    if h >= 2:
                        pe.wait_ge(s_o, t["h0"] + h - 1)
                    for k in range(NB):
                        v = slice(k * P + HD * (h % 2), k * P + HD * (h % 2) + HD)
                        cc, pt = c + (4 if m else 0), slice(4 * k * P, 4 * k * P + (NB - k) * P)
                        ins = mm3(bank[4 + h % 2][0:HD, k * P:S], h_hi[:, cc, v], h_lo[:, cc, v],
                                  bufs["PTh"][:, h % 2, pt], bufs[f"PTl{h % 2}"][:, pt], k == 0, k == NB - 1)
                    ins.then_inc(s_pv, 1)

                scores(0)
                scores(1)
                if m:
                    pe.wait_ge(s_relu, 12 * m)
                scores(2)
                for u in range(nu):
                    if m and u % 4 == 0 and u // 4 < SGU_GROUPS:
                        sgu(m, bufs, u // 4)
                    b = u % 4
                    pe.wait_ge(s_exp, u0 + u + 1)
                    if u >= 2:
                        pe.wait_ge(s_pt, u0 + u - 1)
                    for k in range(b + 1):
                        ins = T.transpose(bank[2 + u % 2][:, k * P:(k + 1) * P], bufs["P"][:, u % 2, k * P:(k + 1) * P], ident)
                    ins.then_inc(s_tr, 1)
                    if u + 3 < nu:
                        scores(u + 3)
                    if u % 4 == 1 and u >= 5:
                        values(u // 4 - 1)
                values(nh - 1)
                if m:
                    pe.wait_ge(s_hlo, H0[f"attn{m}"] + 4)
                pe.wait_ge(s_on, OT0[m] + 1)
                for b in range(NB):
                    ins = T.transpose(bank[6][0:nh, b * P:(b + 1) * P], bufs["fine"][:, 5, b, 0:nh], ident)
                ins.then_inc(s_otr, 1)
                pe.wait_ge(s_sel, m + 1)
                pe.wait_ge(s_cl, m + 1)
                for n in range(nh // 2):
                    if n >= 2:
                        pe.wait_ge(s_on, OT0[m] + n)
                    pick = sel[0:nh, 2 * n:2 * n + 2, :].rearrange("p h d -> p (h d)")
                    T.matmul(bank[7 - n % 2][:], pick, bufs["cTh"][0:nh, :], start=True, stop=False)
                    T.matmul(bank[7 - n % 2][:], pick, bufs["cTl"][0:nh, :], start=False, stop=True).then_inc(s_otr, 1)

            pe.wait_ge(s_const, 32)
            for k in range(KC):
                if k == 0:
                    for b in range(NB):
                        pe.wait_ge(s_xin[b], 16)
                if k >= 4:
                    pe.wait_ge(s_x, k - 3)
                for b in range(NB):
                    ins = T.transpose(bank[k % 4][:, b * P:(b + 1) * P], x_nat[:, b, k * P:(k + 1) * P], ident)
                ins.then_inc(s_xtr, 1)
            pe.wait_ge(s_vecs, 16 * 11)
            T.transpose(bank[4][:, 0:N_VEC], vrows[0:N_VEC, :], ident[0:N_VEC, 0:N_VEC])
            n = N_MOD * KC
            for l in range(2):
                ins = T.transpose(bank[5][:, n * l:n * l + n], brows[0:n, l, :], ident[0:n, 0:n])
            ins.then_inc(s_setup, 1)
            mean(0)
            nb = N0["pool_in"]
            pe.wait_ge(s_x, 8)
            for j in range(4):
                if j >= 2:
                    pe.wait_ge(s_actT, 2 * (j - 1))
                pair(nb + 2 * j, (2 * (j % 2), 2 * (j % 2) + 1), h_hi, h_lo, (s_hlo, H0["n0"]) if j == 0 else None)
            nb = N0["group"]
            pe.wait_ge(s_spread, 1)
            for j in range(2):
                if j:
                    pe.wait_ge(s_actT, 8)
                pe.wait_ge(s_lo, nb + j + 1)
                hi, lo = slab(nb + j, 256)
                for g in range(2):
                    for c in range(2):
                        t = 4 * (1 - j) + 2 * g + c
                        for k in range(2):
                            src = 4 * (1 - j) + 2 * g + k
                            w = 3 - src // 2
                            pe.wait_ge(s_plo, 2 * w + 2)
                            ins = mm3(bank[t][:], hi[:, 2 * g + k, c * P:(c + 1) * P], lo[:, 2 * g + k, c * P:(c + 1) * P],
                                      p_hi[:, src, :], p_lo[:, src, :], k == 0, k == 1)
                ins.then_inc(s_used, 1)
            out_phase("pool_out", act_hi, act_lo, (s_alo, 0), [(s_alo, 4)])
            mean(1)
            ffn(0, "n1")
            mean(2)
            project(0, A1_GROUPS, a1, "n2")
            attention(0)
            out_phase("out0", h_hi, h_lo, (s_hlo, H0["attn0"]), [(s_pt, ATT[1]["u0"]), (s_exp, ATT[1]["u0"])])
            mean(3)
            ffn(1, "n3")
            mean(4)
            mean(5)
            for l in range(2):
                q = 5 + 3 * l
                ffn(2 + 2 * l, ["n5", "n8"][l])
                mean(q + 1)
                project(1 + l, A2_GROUPS, a2, ["n6", "n9"][l])
                attention(1 + l)
                end = ATT[1 + l]["u0"] + ATT[1 + l]["nu"]
                out_phase(f"out{1 + l}", h_hi, h_lo, (s_hlo, H0[f"attn{1 + l}"]), [(s_pt, end), (s_exp, end)])
                mean(q + 2)
                ffn(3 + 2 * l, ["n7", "n10"][l])
                mean(q + 3)
            for b in range(NB):
                for half in range(2):
                    n = 2 * b + half
                    if n == 0:
                        pe.wait_ge(s_x, 8 * 13)
                    if n >= 4:
                        pe.wait_ge(s_ynat, n - 3)
                    for k in range(4):
                        ins = T.transpose(bank[n % 4][:, k * P:(k + 1) * P], yT[:, 4 * half + k, b * P:(b + 1) * P], ident)
                    ins.then_inc(s_ytr, 1)


_INS = ['x', 'norm_mix', 'norm_ffn', 'norm_final', 'pool_w_in', 'pool_w_group', 'pool_scale', 'pool_w_out',
        'attn_w_qkv', 'attn_w_out', 'ffn_w_gate', 'ffn_w_up', 'ffn_w_down', 'c_2', 'positions_2', 'ada_w_2',
        'ada_b_2', 'norm_ffn1_2', 'ffn1_w_in_2', 'ffn1_w_out_2', 'norm_mix_2', 'mix_w_in_2', 'sgu_w_2', 'sgu_b_2',
        'mix_w_out_2', 'norm_ffn2_2', 'ffn2_w_in_2', 'ffn2_w_out_2', 'final_norm_2']
_CONSTS = ['squares', 'rope', 'masks', 'small']


def kernel(**inputs):
    import numpy as _np
    import concourse.bacc as _bacc
    from concourse import mybir as _mybir
    from concourse.bass_utils import run_bass_kernel_spmd as _run

    nc = _bacc.Bacc("TRN2", target_bir_lowering=False, num_devices=1)
    arrays, args = {}, []
    consts = dict(zip(_CONSTS, constants()))
    for name in _INS + _CONSTS:
        a = _np.ascontiguousarray(inputs[name] if name in inputs else consts[name])
        arrays[f"in_{name}_dram"] = a
        args.append(nc.dram_tensor(f"in_{name}_dram", a.shape, _mybir.dt.from_np(a.dtype), kind="ExternalInput").ap())
    out = nc.dram_tensor("out_0_dram", (1, S, D), F32, kind="ExternalOutput").ap()
    program(nc, *args, out)
    r = _run(nc, [arrays], core_ids=[0])
    return r.results[0]["out_0_dram"]
```
